# Optimizing a Trainium2 kernel written in Bass

```python
import jax, jax.numpy as jnp
from jax import lax
import numpy as np

D_MODEL = 1024
BATCH = 1
SEQ = 512
DEPTH = 2

CHUNK = 64
LEFT_CHUNKS = 8
BAND = LEFT_CHUNKS + 1
N_HEADS = 16
HEAD_DIM = D_MODEL // N_HEADS
D_ATT = N_HEADS * HEAD_DIM
REL_CLIP = 128
N_REL = 2 * REL_CLIP + 1
D_RNN = ((4 * D_MODEL // 3 + 127) // 128) * 128
RNN_BLOCKS = 16
RNN_BLOCK_DIM = D_RNN // RNN_BLOCKS
CONV_WIDTH = 4
LRU_C = 8.0
D_FF = ((8 * D_MODEL // 3 + 127) // 128) * 128
EPS = 1e-6
IN_SPLITS = (D_RNN, 2 * D_RNN, 2 * D_RNN + D_ATT, 2 * D_RNN + 2 * D_ATT,
             2 * D_RNN + 3 * D_ATT, 2 * D_RNN + 3 * D_ATT + D_MODEL)
D_IN = 2 * D_RNN + 3 * D_ATT + 2 * D_MODEL

kernel_name = "hybrid_rglru_chunkattn_macaron"

def rms_norm(x, g):
    xf = x.astype(jnp.float32)
    ms = jnp.mean(xf * xf, axis=-1, keepdims=True)
    return (xf * lax.rsqrt(ms + EPS) * g.astype(jnp.float32)).astype(x.dtype)

def swiglu(h, w_gate, w_up, w_down):
    return (jax.nn.silu(h @ w_gate) * (h @ w_up)) @ w_down

def causal_depthwise_conv(x, w, b):
    S = x.shape[1]
    xp = jnp.pad(x, ((0, 0), (CONV_WIDTH - 1, 0), (0, 0)))
    out = b
    for j in range(CONV_WIDTH):
        out = out + xp[:, j:j + S] * w[j]
    return out

def block_diag_linear(x, w, b):
    B, S, _ = x.shape
    xb = x.reshape(B, S, RNN_BLOCKS, RNN_BLOCK_DIM)
    return jnp.einsum('bshi,hij->bshj', xb, w).reshape(B, S, D_RNN) + b

def rg_lru(x, w_a, b_a, w_x, b_x, lam):
    r = jax.nn.sigmoid(block_diag_linear(x, w_a, b_a).astype(jnp.float32))
    i = jax.nn.sigmoid(block_diag_linear(x, w_x, b_x).astype(jnp.float32))
    log_a = -LRU_C * r * jax.nn.softplus(-lam.astype(jnp.float32))
    a = jnp.exp(log_a)
    inp = jnp.sqrt(-jnp.expm1(2.0 * log_a)) * (i * x.astype(jnp.float32))

    def combine(left, right):
        a_l, b_l = left
        a_r, b_r = right
        return a_l * a_r, a_r * b_l + b_r

    _, h = lax.associative_scan(combine, (a, inp), axis=1)
    return h.astype(x.dtype)

def rel_bias_index():
    q_pos = np.arange(CHUNK)[:, None]
    k_pos = np.arange(BAND * CHUNK)[None, :] - LEFT_CHUNKS * CHUNK
    return np.clip(q_pos - k_pos, -REL_CLIP, REL_CLIP) + REL_CLIP

def chunked_attention(q, k, v, rel_table):
    B, S, H, Dh = q.shape
    N = S // CHUNK
    qc = q.reshape(B, N, CHUNK, H, Dh)
    pad = ((0, 0), (LEFT_CHUNKS, 0), (0, 0), (0, 0), (0, 0))
    kp = jnp.pad(k.reshape(B, N, CHUNK, H, Dh), pad)
    vp = jnp.pad(v.reshape(B, N, CHUNK, H, Dh), pad)
    band_idx = np.arange(N)[:, None] + np.arange(BAND)[None, :]
    kb = kp[:, band_idx].reshape(B, N, BAND * CHUNK, H, Dh)
    vb = vp[:, band_idx].reshape(B, N, BAND * CHUNK, H, Dh)
    valid = np.repeat(band_idx >= LEFT_CHUNKS, CHUNK, axis=1)
    bias = rel_table.astype(jnp.float32)[:, rel_bias_index()]
    s = jnp.einsum('bnqhd,bnkhd->bhnqk', qc, kb).astype(jnp.float32) * (HEAD_DIM ** -0.5)
    s = s + bias[None, :, None]
    s = jnp.where(valid[None, None, :, None, :], s, -1e30)
    p = jax.nn.softmax(s, axis=-1).astype(v.dtype)
    o = jnp.einsum('bhnqk,bnkhd->bnqhd', p, vb)
    return o.reshape(B, S, H * Dh)

def setup_inputs(seed: int = 0) -> dict:
    key = jax.random.key(seed)
    ks = jax.random.split(key, 32)
    nrm = lambda k, shape, scale: jax.random.normal(k, shape, jnp.float32) * scale
    gain = lambda k, shape: 1.0 + 0.02 * jax.random.normal(k, shape, jnp.float32)
    u = jax.random.uniform(ks[9], (DEPTH, D_RNN), jnp.float32, minval=0.9, maxval=0.999)
    a0 = u ** (1.0 / LRU_C)
    return {
        "x": nrm(ks[0], (BATCH, SEQ, D_MODEL), 1.0),
        "norm_ffn1": gain(ks[1], (DEPTH, D_MODEL)),
        "ffn1_w_gate": nrm(ks[2], (DEPTH, D_MODEL, D_FF), D_MODEL ** -0.5),
        "ffn1_w_up": nrm(ks[3], (DEPTH, D_MODEL, D_FF), D_MODEL ** -0.5),
        "ffn1_w_down": nrm(ks[4], (DEPTH, D_FF, D_MODEL), D_FF ** -0.5),
        "norm_mix": gain(ks[5], (DEPTH, D_MODEL)),
        "w_in": nrm(ks[6], (DEPTH, D_MODEL, D_IN), D_MODEL ** -0.5),
        "gate_bias": nrm(ks[7], (DEPTH, 2 * D_MODEL), 0.01),
        "conv_w": nrm(ks[8], (DEPTH, CONV_WIDTH, D_RNN), CONV_WIDTH ** -0.5),
        "conv_b": nrm(ks[10], (DEPTH, D_RNN), 0.01),
        "rg_w_a": nrm(ks[11], (DEPTH, RNN_BLOCKS, RNN_BLOCK_DIM, RNN_BLOCK_DIM), RNN_BLOCK_DIM ** -0.5),
        "rg_b_a": nrm(ks[12], (DEPTH, D_RNN), 0.01),
        "rg_w_x": nrm(ks[13], (DEPTH, RNN_BLOCKS, RNN_BLOCK_DIM, RNN_BLOCK_DIM), RNN_BLOCK_DIM ** -0.5),
        "rg_b_x": nrm(ks[14], (DEPTH, D_RNN), 0.01),
        "rg_lambda": jnp.log(a0) - jnp.log1p(-a0),
        "w_up_a": nrm(ks[15], (DEPTH, D_RNN, D_MODEL), D_RNN ** -0.5),
        "q_gain": gain(ks[16], (DEPTH, HEAD_DIM)),
        "k_gain": gain(ks[17], (DEPTH, HEAD_DIM)),
        "rel_table": nrm(ks[18], (DEPTH, N_HEADS, N_REL), 0.1),
        "w_up_b": nrm(ks[19], (DEPTH, D_ATT, D_MODEL), D_ATT ** -0.5),
        "w_out": nrm(ks[20], (DEPTH, D_MODEL, D_MODEL), D_MODEL ** -0.5),
        "norm_ffn2": gain(ks[21], (DEPTH, D_MODEL)),
        "ffn2_w_gate": nrm(ks[22], (DEPTH, D_MODEL, D_FF), D_MODEL ** -0.5),
        "ffn2_w_up": nrm(ks[23], (DEPTH, D_MODEL, D_FF), D_MODEL ** -0.5),
        "ffn2_w_down": nrm(ks[24], (DEPTH, D_FF, D_MODEL), D_FF ** -0.5),
    }

def reference(x, norm_ffn1, ffn1_w_gate, ffn1_w_up, ffn1_w_down, norm_mix, w_in, gate_bias,
              conv_w, conv_b, rg_w_a, rg_b_a, rg_w_x, rg_b_x, rg_lambda, w_up_a,
              q_gain, k_gain, rel_table, w_up_b, w_out,
              norm_ffn2, ffn2_w_gate, ffn2_w_up, ffn2_w_down):
    B, S, _ = x.shape
    for l in range(DEPTH):
        x = x + 0.5 * swiglu(rms_norm(x, norm_ffn1[l]), ffn1_w_gate[l], ffn1_w_up[l], ffn1_w_down[l])

        h = rms_norm(x, norm_mix[l])
        proj = h @ w_in[l]
        xr, yr, q, k, v, g_a, g_b = jnp.split(proj, IN_SPLITS, axis=-1)

        hr = rg_lru(causal_depthwise_conv(xr, conv_w[l], conv_b[l]),
                    rg_w_a[l], rg_b_a[l], rg_w_x[l], rg_b_x[l], rg_lambda[l])
        y_a = (jax.nn.gelu(yr) * hr) @ w_up_a[l]

        qh = rms_norm(q.reshape(B, S, N_HEADS, HEAD_DIM), q_gain[l])
        kh = rms_norm(k.reshape(B, S, N_HEADS, HEAD_DIM), k_gain[l])
        vh = v.reshape(B, S, N_HEADS, HEAD_DIM)
        y_b = chunked_attention(qh, kh, vh, rel_table[l]) @ w_up_b[l]

        gates = jnp.concatenate([g_a, g_b], axis=-1) + gate_bias[l]
        gate_a = jax.nn.sigmoid(gates[..., :D_MODEL])
        gate_b = jax.nn.sigmoid(gates[..., D_MODEL:])
        x = x + (gate_a * y_a + gate_b * y_b) @ w_out[l]

        x = x + 0.5 * swiglu(rms_norm(x, norm_ffn2[l]), ffn2_w_gate[l], ffn2_w_up[l], ffn2_w_down[l])
    return x


_drawn_inputs = setup_inputs


def setup_inputs(seed=0):
    import zlib

    import numpy as np

    out = dict(_drawn_inputs(seed))
    spreads = {}
    factors = {'norm_ffn1': 4.392,
     'norm_mix': 5.79,
     'gate_bias': 8.0,
     'rg_b_a': 23.293,
     'rg_b_x': 8.0,
     'q_gain': 8.0,
     'k_gain': 8.0,
     'rel_table': 7.362,
     'norm_ffn2': 4.984,
     'conv_b': 3.129}
    for name, (base, spread) in spreads.items():
        noise = np.random.default_rng([zlib.crc32(name.encode()), seed]).standard_normal(out[name].shape)
        drawn = base * np.exp(spread * noise) if base else spread * noise
        out[name] = __import__('jax').numpy.asarray(drawn.astype(out[name].dtype))
    for name, factor in factors.items():
        out[name] = (out[name] * factor).astype(out[name].dtype)
    return out
```

```python
from contextlib import ExitStack

import numpy as np
import concourse.bass as bass
from concourse import mybir

F32, F32R = mybir.dt.float32, mybir.dt.float32r
ACT, ALU = mybir.ActivationFunctionType, mybir.AluOpType

P = 128
D, S, DEPTH = 1024, 512, 2
HEADS, HD, CHUNK = 16, 64, 64
REL_CLIP, CONV, LRU_C, EPS = 128, 4, 8.0, 1e-6
RNN = ((4 * D // 3 + P - 1) // P) * P
RB = RNN // 16
FF = ((8 * D // 3 + P - 1) // P) * P
KD, KR, KF, KS = D // P, RNN // P, FF // P, S // P
PAIR = 2 * P
TURNS = FF // PAIR
SLOTS, AHEAD = 4, 3
CW = 4 * PAIR

XR0, YR0, Q0 = 0, RNN, 2 * RNN
K0, V0, G0 = Q0 + D, Q0 + 2 * D, Q0 + 3 * D

BANDS = [(m, g, k) for m in range(KR) for g in range(2) for k in (m - 1, m, m + 1) if 0 <= k < KR]
BPC = CW // P
RG_CHUNKS = -(-len(BANDS) // BPC)

G8 = [(0, 4), (4, 8)]
G22 = [(0, 4), (4, 8), (8, 12), (12, 16), (16, 20), (20, 22)]
G11A = [(0, 4), (4, 8), (8, 11)]
G11B = [(0, 3), (3, 6), (6, 9), (9, 11)]
UP_A = [G11A, G11A, G11B, G11B]
XR_CHUNKS = (KR // 2) * len(G8) + 1
FFN_CHUNKS = TURNS * 4 + (KD // 2) * len(G22)
MIX_CHUNKS = 2 * XR_CHUNKS + RG_CHUNKS + sum(map(len, UP_A)) + 2 * KD + 2 * KD + KD + KD + KD
CHUNKS = 2 * FFN_CHUNKS + MIX_CHUNKS
BEFORE_ATTENTION = FFN_CHUNKS + MIX_CHUNKS - 2 * KD

PAR, NPAR = {}, 0
for _name, _n in (("ffn1", KD), ("mix", KD), ("ffn2", KD), ("gate", 2 * KD), ("conv_w", CONV * KR), ("conv_b", KR),
                  ("b_a", KR), ("b_x", KR), ("lam", KR), ("q_gain", 1), ("k_gain", 1)):
    PAR[_name] = NPAR
    NPAR += _n

RELW = 2 * REL_CLIP + 1
RELPAD = 3 * P - 1
RELROW = 5 * P

TURNED = [(4, 0, KS * P, (0,)), (5, KS * P, KS * P, (1, 3)), (7, 2 * KS * P, 2 * P, (2,))]

HALF_LN2 = 0.5 * float(np.log(2.0))
TINY = 1e-37

PER_TURN = {"hi_made": 4, "lo_made": 4, "chunk_begun": 4, "for_act": 2, "for_dve": 2, "split_hi": 2, "split_lo": 2,
            **{f"bank_read{b}": 1 for b in range(4)}, **{f"raw_loaded{s}": 16 for s in range(SLOTS)}}
PER_LAYER = {
    "hi_made": CHUNKS, "lo_made": CHUNKS, "chunk_begun": CHUNKS, "for_act": 184, "for_dve": 148,
    "square_made": 3 * KD + 2 * KD, "square_used": 3 * KD + 2 * KD, "rstd_made": 3,
    "to_split": 3 * KD + KR + KD, "split_hi": 106, "split_lo": 98,
    "conv_begun": KR, "gated": KR, "tanh_made": KR, "logs_made": KR, "diff_made": KR, "drive_made": KR,
    "conv_step": 2 * KR, "scan_step": 2 * KR, "soft_step": 18, "lam_exp": 1, "decay_made": 1,
    "ga_used": KD, "qk_made": 2 * KD, "qk_rstd": 2 * KD, "band_masked": 1, "q_placed": HEADS + 2,
    "exp_made": HEADS * KS, "prob_made": HEADS * KS, "inv_made": HEADS,
    "bank_read0": 49, "bank_read1": 46, "bank_read2": 56, "bank_read3": 56, "bank_read4": 38, "bank_read5": 38,
    "bank_read6": 30, "bank_read7": 38,
    **{f"raw_loaded{s}": 16 * CHUNKS // SLOTS for s in range(SLOTS)},
    "band_loaded0": 16 * HEADS, "band_loaded1": 16 * HEADS, "par_loaded": 16}


class Count:

    def __init__(self, start):
        self.n, self.loops = start, {}

    def value(self):
        v = self.n
        for reg, per in self.loops.values():
            v = reg * per + v
        return v


class Counts:

    def __init__(self, sems, starts):
        self.names = {id(s): n for n, s in sems.items()}
        self.all = {n: Count(starts.get(n, 0)) for n in sems}
        self.open = {}

    def step(self, sem, by=1):
        self.all[self.names[id(sem)]].n += by

    def made(self, sem, by=1):
        self.step(sem, by)
        return by

    def now(self, sem, back=0):
        self.step(sem, -back)
        v = self.all[self.names[id(sem)]].value()
        self.step(sem, back)
        return v

    def next(self, sem, by=1):
        self.step(sem, by)
        return self.now(sem)

    def enter(self, kind, table, reg, first=0):
        self.open[kind] = (table, first, {n: c.n for n, c in self.all.items()})
        for n, c in self.all.items():
            c.loops[kind] = (reg, table.get(n, 0))
            c.n -= first * table.get(n, 0)

    def leave(self, kind, passes):
        table, first, before = self.open.pop(kind)
        for n, c in self.all.items():
            per = table.get(n, 0)
            made = c.n + first * per - before[n]
            assert made in (0, per), (kind, n, made, per)
            c.n = before[n] + made * (passes - first)
            del c.loops[kind]


def trunk(nc, x_in, w_gate1, w_up1, w_down1, w_in, rg_band, w_up_a, w_up_b, w_out, w_gate2, w_up2, w_down2,
          params, rel_rev, out):
    rel_rows = nc.dram_tensor("rel_rows", (DEPTH * HEADS, RELROW), F32)
    rel_band = nc.dram_tensor("rel_band", (DEPTH * HEADS, P, S), F32)

    ctx = ExitStack()
    with ctx:
        def sb(name, shape, dt=F32):
            return ctx.enter_context(nc.sbuf_tensor(name, shape, dt))

        def sem(name):
            return ctx.enter_context(nc.semaphore(name))

        x = sb("x", [P, KD, S])
        h_hi, h_lo = sb("h_hi", [P, KD, S], F32R), sb("h_lo", [P, KD, S], F32R)
        raw = sb("raw", [P, SLOTS, CW])
        whi, wlo = sb("whi", [P, SLOTS, CW], F32R), sb("wlo", [P, SLOTS, CW], F32R)
        tmp = sb("tmp", [P, 2, S])
        square = sb("square", [P, 2, S])
        rstd = square[:, 0, :]
        ident, ones, ones_head = sb("ident", [P, P]), sb("ones", [P, P]), sb("ones_head", [P, P])
        par = sb("par", [P, NPAR])
        decay = sb("decay", [P, 2, KR])
        soft = sb("soft", [P, 4, KR])
        qg = sb("qg", [P, 1])
        carrier = sb("carrier", [1, HEADS * KS])
        mx, total, inv = sb("mx", [P, 2, KS]), sb("total", [P, 2, KS]), sb("inv", [P, 2, KS])

        def views(*parts):
            made = []
            with ExitStack() as scope:
                for n, (name, shape, dt) in enumerate(parts):
                    made.append(scope.enter_context(nc.sbuf_tensor(name, shape, dt)))
            return made

        R = KR * S
        act_hi, act_lo, gate, _ = views(("act_hi", [P, KF, S], F32R), ("act_lo", [P, KF, S], F32R),
                                        ("gate", [P, 2, S], F32), ("pad_f", [P, 2048], F32))
        u, u_hi, u_lo, r = views(("u", [P, KR, S], F32), ("u_hi", [P, KR, S], F32R), ("u_lo", [P, KR, S], F32R),
                                 ("r", [P, KR, S], F32))
        _, scan, y = views(("pad_a", [P, R], F32), ("scan", [P, KR, S], F32), ("y", [P, KR, S], F32))
        ya_hi, _, ya_lo = views(("ya_hi", [P, KR, S], F32R), ("pad_b", [P, 2 * R], F32), ("ya_lo", [P, KR, S], F32R))
        TRI = P * (KS * (KS + 1) // 2)
        q, v3, _, ya_out, pt, _, gb_out, p0, _, k, p1, _, v012 = views(
            ("q", [P, KD, S], F32), ("v3", [P, D], F32), ("pad_c", [P, R - KD * S - D], F32),
            ("ya_out", [P, KD, S], F32), ("pt", [P, TRI], F32), ("pad_d", [P, R - KD * S - TRI], F32),
            ("gb_out", [P, KD, S], F32), ("p0", [P, TRI], F32), ("pad_e", [P, R - KD * S - TRI], F32),
            ("k", [P, KD, S], F32), ("p1", [P, TRI], F32), ("pad_g", [P, R - KD * S - TRI], F32),
            ("v012", [P, 3, D], F32))
        m_hi, _, m_lo = views(("m_hi", [P, KD, S], F32R), ("pad_h", [P, 3 * R - KD * S], F32),
                              ("m_lo", [P, KD, S], F32R))
        x_tok, rel_t = views(("x_tok", [P, KS, D], F32), ("rel_t", [DEPTH * HEADS, RELROW], F32))
        y_tok, = views(("y_tok", [P, KS, D], F32))
        prob = [p0, p1]
        qk = [q, k]
        v = [v012[:, 0, :], v012[:, 1, :], v012[:, 2, :], v3[:, :]]

        ps = ctx.enter_context(nc.psum_tensor("ps", [P, 8, S], F32))

        hi_made, lo_made, chunk_begun = sem("hi_made"), sem("lo_made"), sem("chunk_begun")
        raw_loaded = [sem(f"raw_loaded{s}") for s in range(SLOTS)]
        for_act, for_dve = sem("for_act"), sem("for_dve")
        bank_read = [sem(f"bank_read{b}") for b in range(8)]
        square_made, square_used, rstd_made = sem("square_made"), sem("square_used"), sem("rstd_made")
        to_split, split_hi, split_lo = sem("to_split"), sem("split_hi"), sem("split_lo")
        conv_begun, conv_step, gated, tanh_made = sem("conv_begun"), sem("conv_step"), sem("gated"), sem("tanh_made")
        logs_made, diff_made, drive_made = sem("logs_made"), sem("diff_made"), sem("drive_made")
        scan_step, soft_step, lam_exp, decay_made = sem("scan_step"), sem("soft_step"), sem("lam_exp"), sem("decay_made")
        ga_used, qk_made, qk_rstd = sem("ga_used"), sem("qk_made"), sem("qk_rstd")
        exp_made, prob_made, inv_made, band_masked = sem("exp_made"), sem("prob_made"), sem("inv_made"), sem("band_masked")
        q_placed = sem("q_placed")
        band_loaded = [sem(f"band_loaded{n}") for n in range(2)]
        par_loaded = sem("par_loaded")
        counted = {
            "hi_made": hi_made, "lo_made": lo_made, "chunk_begun": chunk_begun, "for_act": for_act,
            "for_dve": for_dve, "square_made": square_made, "square_used": square_used, "rstd_made": rstd_made,
            "to_split": to_split, "split_hi": split_hi, "split_lo": split_lo, "conv_begun": conv_begun,
            "conv_step": conv_step, "gated": gated, "tanh_made": tanh_made, "logs_made": logs_made,
            "diff_made": diff_made, "drive_made": drive_made, "scan_step": scan_step, "soft_step": soft_step,
            "lam_exp": lam_exp, "decay_made": decay_made, "ga_used": ga_used, "qk_made": qk_made,
            "qk_rstd": qk_rstd, "exp_made": exp_made, "prob_made": prob_made, "inv_made": inv_made,
            "band_masked": band_masked, "q_placed": q_placed, "par_loaded": par_loaded,
            **{f"bank_read{b}": bank_read[b] for b in range(8)},
            **{f"raw_loaded{s}": raw_loaded[s] for s in range(SLOTS)},
            **{f"band_loaded{n}": band_loaded[n] for n in range(2)}}
        par_free = sem("par_free")
        x_loaded, rel_loaded, rel_padded, rel_stored, consts_made = (
            sem("x_loaded"), sem("rel_loaded"), sem("rel_padded"), sem("rel_stored"), sem("consts_made"))
        out_made, out_stored = sem("out_made"), sem("out_stored")

        STARTS = {"lo_made": SLOTS}

        def counts(**starts):
            return Counts(counted, {**STARTS, **starts})

        def mix_bank(n):
            return 2 + n % 6

        XR_T, RG_T, YR_T, UA_T, G_T, QK_T, V_T, UB_T, OUT_T = np.cumsum(
            [0, KR, 2 * KR, KR, KD, 2 * KD, 2 * KD, KD, KD]).tolist()

        block = ctx.enter_context(nc.Block())

        @block.sync
        def _(sp):
            C = counts(lo_made=0)
            place = [0]

            def load(src, shape):
                s = place[0] % SLOTS
                place[0] += 1
                sp.wait_ge(lo_made, C.next(lo_made))
                n = int(np.prod(shape))
                dst = raw[:, s, 0:n].rearrange("p (a b) -> p a b", a=shape[0]) if len(shape) == 2 else raw[:, s, 0:n]
                sp.dma_start(dst, src).then_inc(raw_loaded[s], 16)

            def rows(w, kt):
                return w.rearrange("l (k p) n -> p (l k) n", p=P)

            def pairs(w, kt, l, col, n_pairs, groups):
                v_ = rows(w, kt)
                for j in range(n_pairs):
                    for a, b in (groups[j] if isinstance(groups[0], list) else groups):
                        load(v_[:, bass.ds(l * kt + a, b - a), col + j * PAIR:col + (j + 1) * PAIR], (b - a, PAIR))

            def ffn(w_gate, w_up, w_down, l):
                g_, u_ = rows(w_gate, KD), rows(w_up, KD)
                with sp.Fori(0, TURNS) as i:
                    C.enter("turn", PER_TURN, i)
                    for w in (g_, u_):
                        for a, b in G8:
                            load(w[:, bass.ds(l * KD + a, 4), bass.ds(i * PAIR, PAIR)], (4, PAIR))
                    C.leave("turn", TURNS)
                pairs(w_down, KF, l, 0, KD // 2, G22)

            sp.dma_start(x_tok[:, :, :], x_in.rearrange("b (t p) d -> p (b t) d", p=P)).then_inc(x_loaded, 16)
            sp.dma_start(rel_t[:, RELPAD:RELPAD + RELW], rel_rev).then_inc(rel_loaded, 16)

            with sp.Fori(0, DEPTH) as l:
                C.enter("layer", PER_LAYER, l)
                sp.wait_ge(par_free, l + 1)
                sp.dma_start(par[:, :].rearrange("p (a n) -> p a n", a=1),
                             params.rearrange("l p n -> p l n")[:, bass.ds(l, 1), :]).then_inc(par_loaded, 16)
                ffn(w_gate1, w_up1, w_down1, l)
                win = rows(w_in, KD)
                for base, band in ((XR0, False), (0, True), (YR0, False)):
                    if band:
                        bands = rg_band.rearrange("l p n -> p l n")
                        for c in range(RG_CHUNKS):
                            n = min(CW, len(BANDS) * P - c * CW)
                            load(bands[:, bass.ds(l, 1), c * CW:c * CW + n], (1, n))
                    else:
                        pairs(w_in, KD, l, base, KR // 2, G8)
                        load(win[:, bass.ds(l * KD, KD), base + (KR - 1) * P:base + KR * P], (KD, P))
                pairs(w_up_a, KR, l, 0, KD // 2, UP_A)
                pairs(w_in, KD, l, G0, KD, G8)
                pairs(w_in, KD, l, Q0, KD, G8)
                for half in range(2):
                    for a in range(0, KD, 2):
                        load(win[:, bass.ds(l * KD + a, 2), V0 + half * S:V0 + (half + 1) * S], (2, S))
                pairs(w_up_b, KD, l, 0, 2, G8)
                sp.wait_ge(band_masked, C.next(band_masked))
                sp.wait_ge(rel_stored, 32)
                for head in range(HEADS):
                    if head >= 2:
                        sp.wait_ge(exp_made, C.next(exp_made, KS))
                    band = rel_band[:, :, :].rearrange("h p n -> p h n")[:, bass.ds(l * HEADS + head, 1), :]
                    for p_, w_ in ((0, S - CHUNK), (CHUNK, S)):
                        sp.dma_start(tmp[p_:p_ + CHUNK, head % 2, 0:w_].rearrange("p (a n) -> p a n", a=1),
                                     band[p_:p_ + CHUNK, :, 0:w_]).then_inc(band_loaded[head % 2], 16)
                C.step(exp_made, 2 * KS)
                v_ = rows(w_up_b, KD)
                for j in range(2, KD // 2):
                    for a, b in G8:
                        load(v_[:, bass.ds(l * KD + a, b - a), j * PAIR:(j + 1) * PAIR], (b - a, PAIR))
                pairs(w_out, KD, l, 0, KD // 2, G8)
                ffn(w_gate2, w_up2, w_down2, l)
                C.leave("layer", DEPTH)
            for _ in range(AHEAD):
                load(rows(w_up_b, KD)[:, 0:4, 0:PAIR], (4, PAIR))
            sp.wait_ge(out_made, 2 * KS)
            sp.dma_start(out.rearrange("b (t p) d -> p (b t) d", p=P), y_tok[:, :, :]).then_inc(out_stored, 16)
            sp.wait_ge(out_stored, 16)

        @block.gpsimd
        def _(pool):
            C = counts()
            nc.gpsimd.memset(soft[:, 0, :], 0.0).then_inc(chunk_begun, AHEAD)
            nc.gpsimd.memset(soft[:, 1, :], 0.0).then_inc(square_used, 2)
            nc.gpsimd.memset(soft[:, 2, :], 0.0).then_inc(par_free, 1)
            nc.gpsimd.memset(ident[:, :], 0.0).then_inc(consts_made, 1)
            nc.gpsimd.memset(ones[:, :], 1.0).then_inc(lo_made, SLOTS)
            nc.gpsimd.memset(ones_head[:, :], 0.0).then_inc(consts_made, 1)
            pool.wait_ge(consts_made, 2)
            nc.gpsimd.affine_select(out=ident[:, :], in_=ident[:, :], compare_op=ALU.not_equal, fill=1.0, base=0,
                                    pattern=[[-1, P]], channel_multiplier=1).then_inc(consts_made, 1)
            nc.gpsimd.memset(ones_head[0:HD, 0:HD], 1.0).then_inc(consts_made, 1)
            pool.wait_ge(consts_made, 4)
            nc.gpsimd.memset(ones_head[HD:P, HD:P], 1.0).then_inc(consts_made, 1)
            pool.wait_ge(consts_made, 5)

            def lo(c, s):
                pool.wait_ge(hi_made, c + 1)
                nc.gpsimd.tensor_tensor(wlo[:, s, :], raw[:, s, :], whi[:, s, :].bitcast(F32),
                                        ALU.subtract).then_inc(lo_made, 1)

            for c in range(AHEAD):
                lo(c, c)
            with pool.Fori(0, DEPTH) as l:
                C.enter("layer", PER_LAYER, l)
                with pool.Fori(0, BEFORE_ATTENTION // SLOTS) as n:
                    for s in range(SLOTS):
                        lo(l * CHUNKS + n * SLOTS + (AHEAD + s), (AHEAD + s) % SLOTS)
                pool.wait_ge(qk_made, C.next(qk_made, 2 * KD))
                for head in range(HEADS):
                    if head >= 2:
                        pool.wait_ge(prob_made, C.next(prob_made, KS))
                    if head:
                        pool.wait_ge(q_placed, C.now(q_placed))
                    p_ = head % 2 * HD
                    zeros = ones_head[p_:p_ + HD, HD - p_:HD - p_ + 1].to_broadcast([HD, S])
                    nc.gpsimd.tensor_tensor(square[p_:p_ + HD, head % 2, :], q[p_:p_ + HD, head // 2, :], zeros,
                                            ALU.add).then_inc(q_placed, C.made(q_placed))
                    if head < 2:
                        nc.gpsimd.tensor_tensor(square[p_:p_ + HD, 1 - head % 2, :], zeros, zeros, ALU.add
                                                ).then_inc(q_placed, C.made(q_placed))
                C.step(prob_made, 2 * KS)
                with pool.Fori(0, (CHUNKS - BEFORE_ATTENTION) // SLOTS) as n:
                    for s in range(SLOTS):
                        lo(l * CHUNKS + n * SLOTS + (BEFORE_ATTENTION + AHEAD + s), (AHEAD + s) % SLOTS)
                C.leave("layer", DEPTH)

        @block.scalar
        def _(act):
            C = counts()
            place = [0]

            def ring(n=1):
                for _ in range(n):
                    s = place[0] % SLOTS
                    place[0] += 1
                    act.wait_ge(chunk_begun, C.next(chunk_begun))
                    act.wait_ge(raw_loaded[s], C.next(raw_loaded[s], 16))
                    nc.scalar.activation(whi[:, s, :], raw[:, s, :], ACT.Copy).then_inc(hi_made, C.made(hi_made))

            def col(name, j=0):
                return par[:, PAR[name] + j:PAR[name] + j + 1]

            def read(b, dst, func, **how):
                act.wait_ge(for_act, C.next(for_act))
                nc.scalar.activation(dst, ps[:, b, :], func, **how).then_inc(bank_read[b], C.made(bank_read[b]))

            def hi_of(dst, src):
                act.wait_ge(to_split, C.next(to_split))
                nc.scalar.activation(dst, src, ACT.Copy).then_inc(split_hi, C.made(split_hi))

            def squared(t, src):
                act.wait_ge(square_used, C.next(square_used))
                nc.scalar.activation(square[:, t % 2, :], src, ACT.Square).then_inc(square_made, C.made(square_made))

            def summed(ahead):
                C.step(square_used, ahead)
                act.wait_ge(square_used, C.now(square_used))
                C.step(square_used, -ahead)

            def norm():
                act.preload_act_table_set("natural_log_exp_and_others")
                summed(2)
                nc.scalar.activation(rstd, ps[:, 0, :], ACT.Ln, scale=1.0 / D, bias=EPS
                    ).then_inc(bank_read[0], C.made(bank_read[0]))
                act.wait_ge(bank_read[0], C.now(bank_read[0]))
                nc.scalar.activation(rstd, rstd, ACT.Exp, scale=-0.5).then_inc(rstd_made, C.made(rstd_made))
                for t in range(KD):
                    hi_of(h_hi[:, t, :], tmp[:, t % 2, :])

            def ffn():
                with act.Fori(0, TURNS) as i:
                    C.enter("turn", PER_TURN, i)
                    ring(2)
                    for m in range(2):
                        read(m, gate[:, m, :], ACT.Silu)
                    ring(2)
                    for m in range(2):
                        C.step(bank_read[2 + m])
                        act.wait_ge(bank_read[2 + m], C.now(bank_read[2 + m]))
                        nc.scalar.activation(
                            act_hi[:, :, :].rearrange("p k s -> p (k s)")[:, bass.ds((i * 2 + m) * S, S)],
                            tmp[:, m, :], ACT.Copy).then_inc(split_hi, C.made(split_hi))
                    C.leave("turn", TURNS)
                for j in range(KD // 2):
                    ring(len(G22))
                    for t in (2 * j, 2 * j + 1):
                        C.step(bank_read[4 + t % 4])
                        act.wait_ge(bank_read[4 + t % 4], C.now(bank_read[4 + t % 4]))
                        squared(t, x[:, t, :])

            act.wait_ge(rel_padded, 1)
            act.dma_start(rel_rows[:, :], rel_t[:, :]).then_inc(rel_stored, 16)
            act.wait_ge(rel_stored, 16)
            act.dma_start(rel_band[:, :, :], bass.AP(rel_rows, P - 1, [[RELROW, DEPTH * HEADS], [-1, P], [1, S]])
                          ).then_inc(rel_stored, 16)
            for t in range(KD):
                C.step(bank_read[t])
                act.wait_ge(bank_read[t], C.now(bank_read[t]))
                squared(t, x[:, t, :])
            ring(AHEAD)

            with act.Fori(0, DEPTH) as l:
                C.enter("layer", PER_LAYER, l)
                C.step(par_loaded, 16)
                norm()
                C.step(soft_step, 2)
                act.wait_ge(soft_step, C.now(soft_step))
                nc.scalar.activation(soft[:, 1, :], soft[:, 1, :], ACT.Exp, scale=-1.0
                    ).then_inc(lam_exp, C.made(lam_exp))
                C.step(soft_step, 16)
                ffn()
                norm()

                def conv_init(t):
                    act.wait_ge(for_act, C.next(for_act))
                    nc.scalar.activation(
                        u[:, t, :], ps[:, mix_bank(XR_T + t), :], ACT.Identity,
                        scale=col("conv_w", (CONV - 1) * KR + t), bias=col("conv_b", t)
                            ).then_inc(conv_begun, C.made(conv_begun))
                    C.step(bank_read[mix_bank(XR_T + t)])

                def conv_hi(t):
                    act.wait_ge(bank_read[mix_bank(XR_T + t)], C.now(bank_read[mix_bank(XR_T + t)]))
                    nc.scalar.activation(u_hi[:, t, :], u[:, t, :], ACT.Copy).then_inc(split_hi, C.made(split_hi))

                for t in range(0, KR, 2):
                    ring()
                    if t:
                        conv_hi(t - 2)
                        conv_hi(t - 1)
                    if t + 1 < KR:
                        ring()
                        conv_init(t)
                        conv_init(t + 1)
                conv_init(KR - 1)
                conv_hi(KR - 1)

                blocks = chunks = 0
                for m in range(KR):
                    for g in range(2):
                        blocks += sum(b[:2] == (m, g) for b in BANDS)
                        while chunks * BPC < blocks:
                            ring()
                            chunks += 1
                        if g and m >= 2:
                            act.wait_ge(gated, C.next(gated))
                        read(mix_bank(RG_T + 2 * m + g), gate[:, m % 2, :] if g else r[:, m, :], ACT.Sigmoid,
                             bias=col("b_x" if g else "b_a", m))
                act.wait_ge(bank_read[mix_bank(RG_T + 2 * KR - 1)], C.now(bank_read[mix_bank(RG_T + 2 * KR - 1)]))
                act.wait_ge(decay_made, C.next(decay_made))

                for m in range(KR):
                    nc.scalar.activation(scan[:, m, :], r[:, m, :], ACT.Tanh,
                                                               scale=decay[:, 0, m:m + 1]
                                                                   ).then_inc(tanh_made, C.made(tanh_made))
                act.preload_act_table_set("natural_log_exp_and_others")
                act.wait_ge(tanh_made, C.now(tanh_made))
                for m in range(KR + 2):
                    if m >= 2:
                        act.wait_ge(diff_made, C.next(diff_made))
                        nc.scalar.activation(scan[:, m - 2, :], scan[:, m - 2, :], ACT.Exp,
                                                                    scale=0.5, bias=HALF_LN2
                                                                        ).then_inc(drive_made, C.made(drive_made))
                    if m < KR:
                        if m == 0:
                            act.wait_ge(gated, C.next(gated, 2))
                        nc.scalar.activation(gate[:, m % 2, :], scan[:, m, :], ACT.Ln, bias=1.0)
                        nc.scalar.activation(scan[:, m, :], scan[:, m, :], ACT.Ln, bias=TINY
                            ).then_inc(logs_made, C.made(logs_made))
                        nc.scalar.activation(r[:, m, :], r[:, m, :], ACT.Exp, scale=decay[:, 1, m:m + 1])
                    if m in (3, 7, 10, 12):
                        ring()

                def gelu(t):
                    read(mix_bank(YR_T + t), y[:, t, :], ACT.Gelu_apprx_tanh)

                done = 0
                for t in range(KR):
                    if t >= 4 and t % 2 == 0:
                        ring(2 if t + 1 < KR else 1)
                    gelu(t)
                    if t % 2 and t >= 5:
                        for _ in range(3):
                            hi_of(ya_hi[:, done, :], tmp[:, done % 2, :])
                            done += 1
                while done < KR:
                    hi_of(ya_hi[:, done, :], tmp[:, done % 2, :])
                    done += 1

                for j in range(KD // 2):
                    ring(len(UP_A[j]))
                    for t in (2 * j, 2 * j + 1):
                        read(mix_bank(UA_T + t), ya_out[:, t, :], ACT.Copy)
                for t in range(2 * KD):
                    if t % 2 == 0:
                        ring(2)
                    if 2 <= t < KD:
                        act.wait_ge(ga_used, C.next(ga_used))
                    read(mix_bank(G_T + t), gate[:, t % 2, :] if t < KD else gb_out[:, t - KD, :], ACT.Sigmoid,
                         bias=col("gate", t))

                act.preload_act_table_set("natural_log_exp_and_others")

                def head_rstd(t, ahead):
                    act.wait_ge(ga_used if t < 2 else qk_made, C.next(ga_used if t < 2 else qk_made))
                    summed(ahead)
                    nc.scalar.activation(gate[:, t % 2, :], ps[:, t % 2, :], ACT.Ln,
                                                              scale=1.0 / HD, bias=EPS
                            ).then_inc(bank_read[t % 2], C.made(bank_read[t % 2]))
                    act.wait_ge(bank_read[t % 2], C.now(bank_read[t % 2]))
                    nc.scalar.activation(gate[:, t % 2, :], gate[:, t % 2, :], ACT.Exp,
                                                             scale=-0.5).then_inc(qk_rstd, C.made(qk_rstd))

                for t in range(0, 2 * KD, 2):
                    ring(2)
                    for n in (t, t + 1):
                        b = mix_bank(QK_T + n)
                        act.wait_ge(for_act, C.next(for_act))
                        squared(n, ps[:, b, :])
                        nc.scalar.activation(qk[n // KD][:, n % KD, :], ps[:, b, :], ACT.Copy
                            ).then_inc(bank_read[b], C.made(bank_read[b]))
                    if t:
                        head_rstd(t - 2, -1)
                        head_rstd(t - 1, 0)
                head_rstd(2 * KD - 2, 1)
                head_rstd(2 * KD - 1, 2)
                C.step(qk_made, 2)

                ring(8)
                for n in range(2 * KS):
                    C.step(bank_read[mix_bank(V_T + n)])

                def exps(head):
                    for i in range(KS):
                        C.step(bank_read[i])
                        act.wait_ge(bank_read[i], C.now(bank_read[i]))
                        part = prob[head % 2][:, tri(i):tri(i + 1)]
                        nc.scalar.activation(part, part, ACT.Exp, scale=-1.0,
                                                                  bias=mx[:, head % 2, i:i + 1],
                                                                  accum_out=total[:, head % 2, i:i + 1]
                                                                      ).then_inc(exp_made, C.made(exp_made))

                exps(0)
                exps(1)
                for head in range(HEADS):
                    for b, at, width, _ in TURNED:
                        act.wait_ge(for_act, C.next(for_act))
                        nc.scalar.activation(pt[:, at:at + width], ps[:, b, 0:width], ACT.Copy
                                             ).then_inc(bank_read[b], C.made(bank_read[b]))
                    if head + 2 < HEADS:
                        exps(head + 2)
                    if head % 2:
                        act.wait_ge(for_act, C.next(for_act))
                        nc.scalar.activation(h_hi[:, head // 2, :], ps[:, 6, :], ACT.Copy
                                             ).then_inc(split_hi, C.made(split_hi))
                        C.step(bank_read[6])

                for t in range(KD):
                    if t % 2 == 0:
                        ring(2)
                    C.step(bank_read[mix_bank(UB_T + t)])
                    hi_of(m_hi[:, t, :], tmp[:, t % 2, :])
                for t in range(KD):
                    if t % 2 == 0:
                        ring(2)
                    C.step(bank_read[mix_bank(OUT_T + t)])
                    act.wait_ge(bank_read[mix_bank(OUT_T + t)], C.now(bank_read[mix_bank(OUT_T + t)]))
                    squared(t, x[:, t, :])
                norm()
                ffn()
                C.leave("layer", DEPTH)

            for t in range(KS):
                act.wait_ge(for_act, C.next(for_act))
                nc.scalar.activation(y_tok[:, t, 0:S], ps[:, 2 * t, :], ACT.Copy).then_inc(out_made, 1)

        @block.vector
        def _(dve):
            C = counts(square_used=2)

            def col(name, j=0):
                return par[:, PAR[name] + j:PAR[name] + j + 1]

            def lo_of(dst, src, hi):
                dve.wait_ge(split_hi, C.next(split_hi))
                nc.vector.tensor_tensor(dst, src, hi.bitcast(F32), ALU.subtract).then_inc(split_lo, C.made(split_lo))

            def added(t):
                dve.wait_ge(square_made, C.next(square_made, 2 if t == 1 else 1))
                if t > 1:
                    dve.wait_ge(square_used, C.now(square_used))
                nc.vector.tensor_tensor(square[:, t % 2, :], square[:, t % 2, :], square[:, (t + 1) % 2, :],
                                        ALU.add).then_inc(square_used, C.made(square_used))

            def squares_behind(t):
                if 2 <= t < KD - 1:
                    added(t - 1)
                if t == KD - 2:
                    added(t)
                if t == KD - 1:
                    C.step(square_made)
                    C.step(square_used, 2)

            def norm(name):
                C.step(bank_read[0])
                dve.wait_ge(rstd_made, C.next(rstd_made))

                def scaled(t):
                    nc.vector.scalar_tensor_tensor(
                        tmp[:, t % 2, :], x[:, t, :], col(name, t), rstd, ALU.mult, ALU.mult
                            ).then_inc(to_split, C.made(to_split))

                scaled(0)
                scaled(1)
                for t in range(KD):
                    lo_of(h_lo[:, t, :], tmp[:, t % 2, :], h_hi[:, t, :])
                    if t + 2 < KD:
                        dve.wait_ge(split_lo, C.now(split_lo))
                        scaled(t + 2)

            def ffn():
                with dve.Fori(0, TURNS) as i:
                    C.enter("turn", PER_TURN, i)
                    for m in range(2):
                        C.step(bank_read[m])
                        dve.wait_ge(bank_read[m], C.now(bank_read[m]))
                        dve.wait_ge(split_lo, C.now(split_lo, 1 - m))
                        dve.wait_ge(for_dve, C.next(for_dve))
                        nc.vector.tensor_tensor(tmp[:, m, :], ps[:, 2 + m, :], gate[:, m, :],
                                                                     ALU.mult
                            ).then_inc(bank_read[2 + m], C.made(bank_read[2 + m]))
                    for m in range(2):
                        at = bass.ds((i * 2 + m) * S, S)
                        lo_of(act_lo[:, :, :].rearrange("p k s -> p (k s)")[:, at], tmp[:, m, :],
                              act_hi[:, :, :].rearrange("p k s -> p (k s)")[:, at])
                    C.leave("turn", TURNS)
                for t in range(KD):
                    dve.wait_ge(for_dve, C.next(for_dve))
                    nc.vector.scalar_tensor_tensor(
                        x[:, t, :], ps[:, 4 + t % 4, :], 0.5, x[:, t, :], ALU.mult, ALU.add
                            ).then_inc(bank_read[4 + t % 4], C.made(bank_read[4 + t % 4]))
                    squares_behind(t)

            dve.wait_ge(rel_loaded, 16)
            nc.vector.tensor_copy(rel_t[:, 0:RELPAD],
                                  rel_t[:, RELPAD:RELPAD + 1].to_broadcast([DEPTH * HEADS, RELPAD])
                                  ).then_inc(rel_padded, 1)
            for t in range(KD):
                dve.wait_ge(for_dve, C.next(for_dve))
                nc.vector.tensor_copy(x[:, t, :], ps[:, t, :]).then_inc(bank_read[t], C.made(bank_read[t]))
                squares_behind(t)

            with dve.Fori(0, DEPTH) as l:
                C.enter("layer", PER_LAYER, l)
                dve.wait_ge(par_loaded, C.next(par_loaded, 16))
                lam = par[:, PAR["lam"]:PAR["lam"] + KR]
                neg, z, c, e = (soft[:, n, :] for n in range(4))
                nc.vector.tensor_scalar(neg, lam, -1.0, None, ALU.mult).then_inc(soft_step, C.made(soft_step))
                dve.wait_ge(soft_step, C.now(soft_step))
                nc.vector.tensor_tensor(z, neg, lam, ALU.max).then_inc(soft_step, C.made(soft_step))
                norm("ffn1")
                dve.wait_ge(lam_exp, C.next(lam_exp))
                nc.vector.tensor_scalar(c, z, 2.0, None, ALU.add).then_inc(soft_step, C.made(soft_step))
                dve.wait_ge(soft_step, C.now(soft_step))
                nc.vector.reciprocal(c, c).then_inc(soft_step, C.made(soft_step))
                dve.wait_ge(soft_step, C.now(soft_step))
                nc.vector.tensor_tensor(z, z, c, ALU.mult).then_inc(soft_step, C.made(soft_step))
                dve.wait_ge(soft_step, C.now(soft_step))
                nc.vector.tensor_tensor(c, z, z, ALU.mult).then_inc(soft_step, C.made(soft_step))
                dve.wait_ge(soft_step, C.now(soft_step))
                nc.vector.tensor_scalar(e, c, 1.0 / 17, None, ALU.mult).then_inc(soft_step, C.made(soft_step))
                dve.wait_ge(soft_step, C.now(soft_step))
                for n in range(15, 1, -2):
                    nc.vector.scalar_tensor_tensor(e, e, 1.0 / n, c, ALU.add, ALU.mult
                        ).then_inc(soft_step, C.made(soft_step))
                    dve.wait_ge(soft_step, C.now(soft_step))
                nc.vector.scalar_tensor_tensor(e, e, 1.0, z, ALU.add, ALU.mult).then_inc(soft_step, C.made(soft_step))
                dve.wait_ge(soft_step, C.now(soft_step))
                nc.vector.tensor_scalar(neg, neg, 0.0, LRU_C, ALU.max, ALU.mult).then_inc(soft_step, C.made(soft_step))
                dve.wait_ge(soft_step, C.now(soft_step))
                nc.vector.scalar_tensor_tensor(decay[:, 0, :], e, 2 * LRU_C, neg, ALU.mult,
                                                                  ALU.add).then_inc(soft_step, C.made(soft_step))
                dve.wait_ge(soft_step, C.now(soft_step))
                nc.vector.tensor_scalar(decay[:, 1, :], decay[:, 0, :], -1.0, None, ALU.mult
                    ).then_inc(soft_step, C.made(soft_step))
                dve.wait_ge(soft_step, C.now(soft_step))
                nc.vector.tensor_scalar(qg[:, :], col("q_gain"), HD ** -0.5, None, ALU.mult
                    ).then_inc(decay_made, C.made(decay_made))
                ffn()
                norm("mix")

                def conv(t):
                    b = mix_bank(XR_T + t)
                    dve.wait_ge(conv_begun, C.next(conv_begun))
                    for back in range(1, CONV):
                        ins = nc.vector.scalar_tensor_tensor(
                            u[:, t, back:S], ps[:, b, 0:S - back], col("conv_w", (CONV - 1 - back) * KR + t),
                            u[:, t, back:S], ALU.mult, ALU.add)
                        if back < CONV - 1:
                            ins.then_inc(conv_step, C.made(conv_step))
                            dve.wait_ge(conv_step, C.now(conv_step))
                        else:
                            ins.then_inc(bank_read[b], C.made(bank_read[b]))

                for t in range(0, KR, 2):
                    both = range(t, min(t + 2, KR))
                    for n in both:
                        conv(n)
                    for n in both:
                        lo_of(u_lo[:, n, :], u[:, n, :], u_hi[:, n, :])
                for m in range(KR):
                    C.step(bank_read[mix_bank(RG_T + 2 * m)])
                    C.step(bank_read[mix_bank(RG_T + 2 * m + 1)])
                    dve.wait_ge(bank_read[mix_bank(RG_T + 2 * m + 1)], C.now(bank_read[mix_bank(RG_T + 2 * m + 1)]))
                    nc.vector.tensor_tensor(u[:, m, :], u[:, m, :], gate[:, m % 2, :], ALU.mult
                        ).then_inc(gated, C.made(gated))
                for m in range(KR + 3):
                    if m < KR:
                        dve.wait_ge(logs_made, C.next(logs_made))
                        nc.vector.tensor_tensor(scan[:, m, :], scan[:, m, :],
                                                                      gate[:, m % 2, :], ALU.subtract
                                                                          ).then_inc(diff_made, C.made(diff_made))
                    if m >= 3:
                        n = m - 3
                        dve.wait_ge(drive_made, C.next(drive_made))
                        nc.vector.tensor_tensor(scan[:, n, :], scan[:, n, :], u[:, n, :],
                                                                   ALU.mult).then_inc(scan_step, C.made(scan_step))
                        dve.wait_ge(scan_step, C.now(scan_step))
                        nc.vector.tensor_tensor_scan(scan[:, n, :], r[:, n, :], scan[:, n, :],
                                                                           0.0, ALU.mult, ALU.add
                                                                               ).then_inc(scan_step, C.made(scan_step))
                dve.wait_ge(scan_step, C.now(scan_step))

                def gated_h(t):
                    b = mix_bank(YR_T + t)
                    C.step(bank_read[b])
                    dve.wait_ge(bank_read[b], C.now(bank_read[b]))
                    nc.vector.tensor_tensor(tmp[:, t % 2, :], y[:, t, :], scan[:, t, :],
                                                                 ALU.mult).then_inc(to_split, C.made(to_split))

                gated_h(0)
                gated_h(1)
                for t in range(KR):
                    lo_of(ya_lo[:, t, :], tmp[:, t % 2, :], ya_hi[:, t, :])
                    if t + 2 < KR:
                        dve.wait_ge(split_lo, C.now(split_lo))
                        gated_h(t + 2)
                dve.wait_ge(split_lo, C.now(split_lo))
                nc.vector.memset(tmp[0:CHUNK, 0, S - CHUNK:S], -1e30)
                nc.vector.memset(tmp[0:CHUNK, 1, S - CHUNK:S], -1e30).then_inc(band_masked, C.made(band_masked))
                for t in range(KD):
                    C.step(bank_read[mix_bank(UA_T + t)])
                for t in range(2 * KD):
                    C.step(bank_read[mix_bank(G_T + t)])
                    if t < KD:
                        dve.wait_ge(bank_read[mix_bank(G_T + t)], C.now(bank_read[mix_bank(G_T + t)]))
                        nc.vector.tensor_tensor(ya_out[:, t, :], ya_out[:, t, :],
                                                                    gate[:, t % 2, :], ALU.mult
                                                                        ).then_inc(ga_used, C.made(ga_used))

                C.step(square_made, 2 * KD)
                C.step(square_used, 2 * KD)

                def qk_scaled(t):
                    C.step(bank_read[t % 2])
                    dve.wait_ge(qk_rstd, C.next(qk_rstd))
                    part = qk[t // KD][:, t % KD, :]
                    nc.vector.scalar_tensor_tensor(
                        part, part, col("k_gain") if t >= KD else qg[:, :], gate[:, t % 2, :], ALU.mult, ALU.mult
                            ).then_inc(qk_made, C.made(qk_made))

                for t in range(2 * KD):
                    C.step(bank_read[mix_bank(QK_T + t)])
                    if t % 2 and t > 1:
                        qk_scaled(t - 3)
                        qk_scaled(t - 2)
                qk_scaled(2 * KD - 2)
                qk_scaled(2 * KD - 1)
                dve.wait_ge(qk_made, C.now(qk_made))
                for half in range(2):
                    for t in range(KS):
                        b = mix_bank(V_T + half * KS + t)
                        dve.wait_ge(for_dve, C.next(for_dve))
                        nc.vector.tensor_copy(v[t][:, half * S:(half + 1) * S], ps[:, b, :]
                            ).then_inc(bank_read[b], C.made(bank_read[b]))

                def biased(head):
                    dve.wait_ge(band_loaded[head % 2], C.next(band_loaded[head % 2], 32))
                    for i in range(KS):
                        dve.wait_ge(for_dve, C.next(for_dve))
                        nc.vector.memset(carrier[0:1, head * KS + i:head * KS + i + 1], 0.0)
                        nc.vector.tensor_tensor_reduce(
                            prob[head % 2][:, tri(i):tri(i + 1)], ps[:, i, 0:(i + 1) * P],
                            tmp[:, head % 2, S - (i + 1) * P:S], -1.0, 3e38, ALU.add, ALU.min,
                            mx[:, head % 2, i:i + 1]).then_inc(bank_read[i], C.made(bank_read[i]))

                def normalised(head):
                    e = head % 2
                    dve.wait_ge(exp_made, C.next(exp_made, KS))
                    nc.vector.reciprocal(inv[:, e, :], total[:, e, :]).then_inc(inv_made, C.made(inv_made))
                    dve.wait_ge(inv_made, C.now(inv_made))
                    for i in range(KS):
                        part = prob[e][:, tri(i):tri(i + 1)]
                        nc.vector.tensor_scalar(part, part, inv[:, e, i:i + 1], None, ALU.mult
                                                ).then_inc(prob_made, C.made(prob_made))

                biased(0)
                biased(1)
                normalised(0)
                for head in range(HEADS):
                    if head + 1 < HEADS:
                        normalised(head + 1)
                    if head + 2 < HEADS:
                        biased(head + 2)
                    for b, *_ in TURNED:
                        C.step(bank_read[b])
                    if head % 2:
                        t = head // 2
                        dve.wait_ge(split_hi, C.next(split_hi))
                        nc.vector.tensor_tensor(h_lo[:, t, :], ps[:, 6, :], h_hi[:, t, :].bitcast(F32), ALU.subtract
                                                ).then_inc(bank_read[6], C.made(bank_read[6]))

                def merged(t):
                    b = mix_bank(UB_T + t)
                    dve.wait_ge(for_dve, C.next(for_dve))
                    nc.vector.tensor_tensor(tmp[:, t % 2, :], ps[:, b, :], gb_out[:, t, :],
                                                             ALU.mult).then_inc(bank_read[b], C.made(bank_read[b]))
                    dve.wait_ge(bank_read[b], C.now(bank_read[b]))
                    nc.vector.tensor_tensor(tmp[:, t % 2, :], tmp[:, t % 2, :],
                                                                 ya_out[:, t, :], ALU.add
                                                                     ).then_inc(to_split, C.made(to_split))

                merged(0)
                merged(1)
                for t in range(KD):
                    lo_of(m_lo[:, t, :], tmp[:, t % 2, :], m_hi[:, t, :])
                    if t + 2 < KD:
                        dve.wait_ge(split_lo, C.now(split_lo))
                        merged(t + 2)
                for t in range(KD):
                    b = mix_bank(OUT_T + t)
                    dve.wait_ge(for_dve, C.next(for_dve))
                    nc.vector.tensor_tensor(x[:, t, :], ps[:, b, :], x[:, t, :], ALU.add
                                            ).then_inc(bank_read[b], C.made(bank_read[b]))
                    squares_behind(t)
                norm("ffn2")
                nc.vector.memset(soft[:, 0, :], 0.0).then_inc(par_free, 1)
                ffn()
                C.leave("layer", DEPTH)

            for t in range(KS):
                dve.wait_ge(for_dve, C.next(for_dve))
                nc.vector.tensor_copy(y_tok[:, t, S:D], ps[:, 2 * t + 1, :]).then_inc(out_made, 1)

        @block.tensor
        def _(pe):
            C = counts()
            place = [0]
            begun = [True]

            def chunk():
                s = place[0] % SLOTS
                place[0] += 1
                pe.wait_ge(lo_made, C.next(lo_made))
                begun[0] = False
                return s

            def product(b, w_hi, w_lo, x_hi, x_lo, start, stop):
                ins = pe.matmul(ps[:, b, :], w_hi, x_lo, start=start, stop=False)
                if not begun[0]:
                    ins.then_inc(chunk_begun, C.made(chunk_begun))
                    begun[0] = True
                pe.matmul(ps[:, b, :], w_hi, x_hi, start=False, stop=False)
                return pe.matmul(ps[:, b, :], w_lo, x_hi, start=False, stop=stop)

            def columns(s, at, m):
                return whi[:, s, at + m * P:at + (m + 1) * P], wlo[:, s, at + m * P:at + (m + 1) * P]

            def pair(groups, kt, banks, hi, lo, ready, wait):
                for g, (a, z) in enumerate(groups):
                    s = chunk()
                    for m, b in enumerate(banks):
                        if g == 0:
                            pe.wait_ge(bank_read[b], C.now(bank_read[b]))
                        for kk in range(a, z):
                            if wait and m == 0:
                                pe.wait_ge(split_lo, C.next(split_lo))
                            ins = product(b, *columns(s, (kk - a) * PAIR, m), hi[:, kk, :], lo[:, kk, :],
                                          kk == 0, kk == kt - 1)
                        if g == len(groups) - 1:
                            ins.then_inc(ready, C.made(ready))
                            C.step(bank_read[b])

            def single(b, hi, lo, ready):
                s = chunk()
                pe.wait_ge(bank_read[b], C.now(bank_read[b]))
                for kk in range(KD):
                    ins = product(b, *columns(s, kk * P, 0), hi[:, kk, :], lo[:, kk, :], kk == 0, kk == KD - 1)
                ins.then_inc(ready, C.made(ready))
                C.step(bank_read[b])

            def summed():
                pe.wait_ge(square_made, C.next(square_made, KD))
                pe.wait_ge(bank_read[0], C.now(bank_read[0]))
                for n in range(2):
                    pe.matmul(ps[:, 0, :], ones[:, :], square[:, n, :], start=n == 0, stop=n == 1
                              ).then_inc(square_used, 1)
                C.step(bank_read[0])

            def ffn():
                def turn(wait):
                    for w in range(2):
                        pair(G8, KD, (2 * w, 2 * w + 1), h_hi, h_lo, for_dve if w else for_act,
                             wait and w == 0)

                turn(True)
                with pe.Fori(1, TURNS) as i:
                    C.enter("turn", PER_TURN, i, 1)
                    turn(False)
                    C.leave("turn", TURNS)
                for j in range(KD // 2):
                    pair(G22, KF, (4 + 2 * (j % 2), 5 + 2 * (j % 2)), act_hi, act_lo, for_dve, j == 0)
                summed()

            pe.wait_ge(consts_made, 5)
            pe.wait_ge(x_loaded, 16)
            for t in range(KD):
                for n in range(KS):
                    ins = pe.transpose(ps[:, t, n * P:(n + 1) * P], x_tok[:, n, t * P:(t + 1) * P], ident[:, :])
                ins.then_inc(for_dve, C.made(for_dve))
                C.step(bank_read[t])
            summed()

            with pe.Fori(0, DEPTH) as l:
                C.enter("layer", PER_LAYER, l)
                ffn()
                for t in range(0, KR - 1, 2):
                    pair(G8, KD, (mix_bank(XR_T + t), mix_bank(XR_T + t + 1)), h_hi, h_lo, for_act, t == 0)
                single(mix_bank(XR_T + KR - 1), h_hi, h_lo, for_act)
                seen = 0
                for n, (m, g, kk) in enumerate(BANDS):
                    if n % BPC == 0:
                        s = chunk()
                    while seen <= kk:
                        pe.wait_ge(split_lo, C.next(split_lo))
                        seen += 1
                    b = mix_bank(RG_T + 2 * m + g)
                    first = n == 0 or BANDS[n - 1][:2] != (m, g)
                    last = n + 1 == len(BANDS) or BANDS[n + 1][:2] != (m, g)
                    if first:
                        pe.wait_ge(bank_read[b], C.now(bank_read[b]))
                    ins = product(b, *columns(s, n % BPC * P, 0), u_hi[:, kk, :], u_lo[:, kk, :], first, last)
                    if last:
                        ins.then_inc(for_act, C.made(for_act))
                        C.step(bank_read[b])
                for t in range(0, KR - 1, 2):
                    pair(G8, KD, (mix_bank(YR_T + t), mix_bank(YR_T + t + 1)), h_hi, h_lo, for_act, False)
                single(mix_bank(YR_T + KR - 1), h_hi, h_lo, for_act)
                for t in range(0, KD, 2):
                    pair(UP_A[t // 2], KR, (mix_bank(UA_T + t), mix_bank(UA_T + t + 1)), ya_hi, ya_lo, for_act,
                         t == 0)
                for t in range(0, 2 * KD, 2):
                    pair(G8, KD, (mix_bank(G_T + t), mix_bank(G_T + t + 1)), h_hi, h_lo, for_act, False)

                def head_sums(t):
                    for n in (t, t + 1):
                        pe.wait_ge(square_made, C.next(square_made))
                        pe.wait_ge(bank_read[n % 2], C.now(bank_read[n % 2]))
                        pe.matmul(ps[:, n % 2, :], ones_head[:, :], square[:, n % 2, :], start=True, stop=True
                                  ).then_inc(square_used, 1)
                        C.step(bank_read[n % 2])

                for t in range(0, 2 * KD, 2):
                    pair(G8, KD, (mix_bank(QK_T + t), mix_bank(QK_T + t + 1)), h_hi, h_lo, for_act, False)
                    if t:
                        head_sums(t - 2)
                head_sums(2 * KD - 2)

                for half in range(2):
                    for a in range(0, KD, 2):
                        s = chunk()
                        for t in range(KS):
                            b = mix_bank(V_T + half * KS + t)
                            if a == 0:
                                pe.wait_ge(bank_read[b], C.now(bank_read[b]))
                            for kk in (a, a + 1):
                                at = (kk - a) * S
                                tok = slice(t * P, (t + 1) * P)
                                w = whi[:, s, at:at + S]
                                ins = pe.matmul(ps[:, b, :], h_lo[:, kk, tok], w, start=kk == 0, stop=False)
                                if not begun[0]:
                                    ins.then_inc(chunk_begun, C.made(chunk_begun))
                                    begun[0] = True
                                pe.matmul(ps[:, b, :], h_hi[:, kk, tok], w, start=False, stop=False)
                                ins = pe.matmul(ps[:, b, :], h_hi[:, kk, tok], wlo[:, s, at:at + S], start=False,
                                                stop=kk == KD - 1)
                            if a == KD - 2:
                                ins.then_inc(for_dve, C.made(for_dve))
                                C.step(bank_read[b])

                for b in range(8):
                    pe.wait_ge(bank_read[b], C.now(bank_read[b]))
                pe.wait_ge(qk_made, C.next(qk_made, 2 * KD))

                def scores(head):
                    t = head // 2
                    if head != 1:
                        pe.wait_ge(q_placed, C.next(q_placed, 1 if head else 4))
                    for i in range(KS):
                        pe.wait_ge(bank_read[i], C.now(bank_read[i]))
                        pe.matmul(ps[:, i, 0:(i + 1) * P], square[:, head % 2, i * P:(i + 1) * P],
                                  k[:, t, 0:(i + 1) * P], start=True, stop=True
                                  ).then_inc(for_dve, C.made(for_dve))
                        C.step(bank_read[i])

                scores(0)
                scores(1)
                for head in range(HEADS):
                    p_ = (head % 2) * HD
                    pe.wait_ge(prob_made, C.next(prob_made, KS))
                    for b, _, _, keys in TURNED:
                        pe.wait_ge(bank_read[b], C.now(bank_read[b]))
                        at = 0
                        for j in keys:
                            for i in range(j, KS):
                                ins = pe.transpose(ps[:, b, at:at + P],
                                                   prob[head % 2][:, tri(i) + j * P:tri(i) + (j + 1) * P], ident[:, :])
                                at += P
                        ins.then_inc(for_act, C.made(for_act))
                        C.step(bank_read[b])
                    if head + 2 < HEADS:
                        scores(head + 2)
                    if head % 2 == 0:
                        pe.wait_ge(bank_read[6], C.now(bank_read[6]))
                    for b, at, _, keys in TURNED:
                        pe.wait_ge(bank_read[b], C.now(bank_read[b]))
                        for j in keys:
                            ins = pe.matmul(ps[p_:p_ + HD, 6, j * P:S], v[j][:, head * HD:(head + 1) * HD],
                                            pt[:, at:at + (KS - j) * P], start=j == 0, stop=j == TURNED[-1][3][-1])
                            at += (KS - j) * P
                    if head % 2:
                        ins.then_inc(for_act, C.made(for_act))
                        C.step(bank_read[6])

                pe.wait_ge(bank_read[6], C.now(bank_read[6]))
                for t in range(0, KD, 2):
                    pair(G8, KD, (mix_bank(UB_T + t), mix_bank(UB_T + t + 1)), h_hi, h_lo, for_dve, False)
                for t in range(0, KD, 2):
                    pair(G8, KD, (mix_bank(OUT_T + t), mix_bank(OUT_T + t + 1)), m_hi, m_lo, for_dve, t == 0)
                summed()
                ffn()
                C.leave("layer", DEPTH)

            for b in range(1, 8):
                pe.wait_ge(bank_read[b], C.now(bank_read[b]))
            for t in range(KS):
                for half in range(2):
                    for n in range(KD // 2):
                        ins = pe.transpose(ps[:, 2 * t + half, n * P:(n + 1) * P],
                                           x[:, half * (KD // 2) + n, t * P:(t + 1) * P], ident[:, :])
                    ins.then_inc(for_dve if half else for_act, C.made(for_dve if half else for_act))


def tri(i):
    return P * (i * (i + 1) // 2)


def kernel(**inputs):
    import concourse.bacc as bacc
    from concourse.bass_utils import run_bass_kernel_spmd as run

    a = {n: np.ascontiguousarray(v) for n, v in inputs.items()}

    def tiles(v):
        return v.reshape(DEPTH, -1, P).transpose(0, 2, 1)

    conv = a["conv_w"].reshape(DEPTH, CONV * RNN)
    params = np.concatenate(
        [tiles(a[n]) for n in ("norm_ffn1", "norm_mix", "norm_ffn2", "gate_bias")] + [tiles(conv)]
        + [tiles(a[n]) for n in ("conv_b", "rg_b_a", "rg_b_x", "rg_lambda")]
        + [np.concatenate([a[n], a[n]], axis=1)[:, :, None] for n in ("q_gain", "k_gain")], axis=2)
    band = np.zeros((DEPTH, P, len(BANDS) * P), np.float32)
    for n, (m, g, kk) in enumerate(BANDS):
        for blk in range(RNN // RB):
            r0, r1 = max(blk * RB, kk * P), min((blk + 1) * RB, (kk + 1) * P)
            c0, c1 = max(blk * RB, m * P), min((blk + 1) * RB, (m + 1) * P)
            if r0 < r1 and c0 < c1:
                w = a["rg_w_x" if g else "rg_w_a"]
                band[:, r0 - kk * P:r1 - kk * P, n * P + c0 - m * P:n * P + c1 - m * P] = \
                    w[:, blk, r0 - blk * RB:r1 - blk * RB, c0 - blk * RB:c1 - blk * RB]
    rel = a["rel_table"][:, :, ::-1].reshape(DEPTH * HEADS, RELW)
    arrays = {
        "x": a["x"], "w_gate1": a["ffn1_w_gate"], "w_up1": a["ffn1_w_up"], "w_down1": a["ffn1_w_down"],
        "w_in": a["w_in"], "rg_band": band, "w_up_a": a["w_up_a"], "w_up_b": a["w_up_b"], "w_out": a["w_out"],
        "w_gate2": a["ffn2_w_gate"], "w_up2": a["ffn2_w_up"], "w_down2": a["ffn2_w_down"], "params": params,
        "rel_rev": rel,
    }
    arrays = {f"in_{n}": np.ascontiguousarray(v) for n, v in arrays.items()}
    nc = bacc.Bacc("TRN2", target_bir_lowering=False, num_devices=1)
    args = [nc.dram_tensor(n, v.shape, mybir.dt.from_np(v.dtype), kind="ExternalInput").ap()
            for n, v in arrays.items()]
    args.append(nc.dram_tensor("out", (1, S, D), F32, kind="ExternalOutput").ap())
    trunk(nc, *args)
    return run(nc, [arrays], core_ids=[0]).results[0]["out"]
```

```python
from contextlib import ExitStack

import numpy as np
import concourse.bass as bass
from concourse import mybir

F32, F32R = mybir.dt.float32, mybir.dt.float32r
ACT, ALU = mybir.ActivationFunctionType, mybir.AluOpType

P = 128
D, S, DEPTH = 1024, 512, 2
HEADS, HD, CHUNK = 16, 64, 64
REL_CLIP, CONV, LRU_C, EPS = 128, 4, 8.0, 1e-6
RNN = ((4 * D // 3 + P - 1) // P) * P
RB = RNN // 16
FF = ((8 * D // 3 + P - 1) // P) * P
KD, KR, KF, KS = D // P, RNN // P, FF // P, S // P
PAIR = 2 * P
TURNS = FF // PAIR
SLOTS, AHEAD = 4, 3
CW = 4 * PAIR

XR0, YR0, Q0 = 0, RNN, 2 * RNN
K0, V0, G0 = Q0 + D, Q0 + 2 * D, Q0 + 3 * D

BANDS = [(m, g, k) for m in range(KR) for g in range(2) for k in (m - 1, m, m + 1) if 0 <= k < KR]
BPC = CW // P
RG_CHUNKS = -(-len(BANDS) // BPC)

G8 = [(0, 4), (4, 8)]
G22 = [(0, 4), (4, 8), (8, 12), (12, 16), (16, 20), (20, 22)]
G11A = [(0, 4), (4, 8), (8, 11)]
G11B = [(0, 3), (3, 6), (6, 9), (9, 11)]
UP_A = [G11A, G11A, G11B, G11B]
XR_CHUNKS = (KR // 2) * len(G8) + 1
FFN_CHUNKS = TURNS * 4 + (KD // 2) * len(G22)
MIX_CHUNKS = 2 * XR_CHUNKS + RG_CHUNKS + sum(map(len, UP_A)) + 2 * KD + 2 * KD + KD + KD + KD
CHUNKS = 2 * FFN_CHUNKS + MIX_CHUNKS
BEFORE_ATTENTION = FFN_CHUNKS + MIX_CHUNKS - 2 * KD

PAR, NPAR = {}, 0
for _name, _n in (("ffn1_next", KD), ("mix", KD), ("ffn2", KD), ("gate", 2 * KD), ("conv_w", CONV * KR), ("conv_b", KR),
                  ("b_a", KR), ("b_x", KR), ("lam", KR), ("q_gain", 1), ("k_gain", 1)):
    PAR[_name] = NPAR
    NPAR += _n

RELW = 2 * REL_CLIP + 1
RELPAD = 3 * P - 1
RELROW = 5 * P

TURNED = [(4, 0, KS * P, (0,)), (5, KS * P, KS * P, (1, 3)), (7, 2 * KS * P, 2 * P, (2,))]

HALF_LN2 = 0.5 * float(np.log(2.0))
TINY = 1e-37

PER_TURN = {"hi_made": 4, "lo_made": 4, "chunk_begun": 4, "for_dve": 4, "silu_made": 2, "to_split": 2,
            "split_hi": 2, "split_lo": 2,
            **{f"bank_read{b}": 1 for b in range(4)}, **{f"raw_loaded{s}": 16 for s in range(SLOTS)}}
PER_LAYER = {
    "hi_made": CHUNKS, "lo_made": CHUNKS, "chunk_begun": CHUNKS, "for_act": 121, "for_dve": 211, "silu_made": 4 * TURNS,
    "square_made": 3 * KD + 2 * KD, "square_used": 3 * KD + 2 * KD, "rstd_made": 3,
    "to_split": 3 * KD + 4 * TURNS + KR + KD, "split_hi": 106, "split_lo": 98,
    "conv_begun": KR, "gated": KR, "tanh_made": KR, "logs_made": KR, "diff_made": KR, "drive_made": KR,
    "conv_step": 2 * KR, "scan_step": 2 * KR, "soft_step": 18, "lam_exp": 1, "decay_made": 1,
    "gelu_made": KR, "qk_made": 2 * KD, "qk_rstd": 2 * KD, "band_masked": 1, "q_placed": HEADS + 2,
    "exp_made": HEADS * KS, "prob_made": HEADS * KS, "inv_made": HEADS,
    "bank_read0": 47, "bank_read1": 46, "bank_read2": 56, "bank_read3": 56, "bank_read4": 40, "bank_read5": 38,
    "bank_read6": 30, "bank_read7": 38,
    **{f"raw_loaded{s}": 16 * CHUNKS // SLOTS for s in range(SLOTS)},
    "band_loaded0": 16 * HEADS, "band_loaded1": 16 * HEADS, "par_loaded": 16}


class Count:

    def __init__(self, start):
        self.n, self.loops = start, {}

    def value(self):
        v = self.n
        for reg, per in self.loops.values():
            v = reg * per + v
        return v


class Counts:

    def __init__(self, sems, starts):
        self.names = {id(s): n for n, s in sems.items()}
        self.all = {n: Count(starts.get(n, 0)) for n in sems}
        self.open = {}

    def step(self, sem, by=1):
        self.all[self.names[id(sem)]].n += by

    def made(self, sem, by=1):
        self.step(sem, by)
        return by

    def now(self, sem, back=0):
        self.step(sem, -back)
        v = self.all[self.names[id(sem)]].value()
        self.step(sem, back)
        return v

    def next(self, sem, by=1):
        self.step(sem, by)
        return self.now(sem)

    def enter(self, kind, table, reg, first=0):
        self.open[kind] = (table, first, {n: c.n for n, c in self.all.items()})
        for n, c in self.all.items():
            c.loops[kind] = (reg, table.get(n, 0))
            c.n -= first * table.get(n, 0)

    def leave(self, kind, passes):
        table, first, before = self.open.pop(kind)
        for n, c in self.all.items():
            per = table.get(n, 0)
            made = c.n + first * per - before[n]
            assert made in (0, per), (kind, n, made, per)
            c.n = before[n] + made * (passes - first)
            del c.loops[kind]


def trunk(nc, x_in, w_gate1, w_up1, w_down1, w_in, rg_band, w_up_a, w_up_b, w_out, w_gate2, w_up2, w_down2,
          params, rel_rev, first_gain, out):
    rel_rows = nc.dram_tensor("rel_rows", (DEPTH * HEADS, RELROW), F32)
    rel_band = nc.dram_tensor("rel_band", (DEPTH * HEADS, P, S), F32)

    ctx = ExitStack()
    with ctx:
        def sb(name, shape, dt=F32):
            return ctx.enter_context(nc.sbuf_tensor(name, shape, dt))

        def sem(name):
            return ctx.enter_context(nc.semaphore(name))

        x = sb("x", [P, KD, S])
        h_hi, h_lo = sb("h_hi", [P, KD, S], F32R), sb("h_lo", [P, KD, S], F32R)
        raw = sb("raw", [P, SLOTS, CW])
        whi, wlo = sb("whi", [P, SLOTS, CW], F32R), sb("wlo", [P, SLOTS, CW], F32R)
        tmp = sb("tmp", [P, 2, S])
        square = sb("square", [P, 2, S])
        rstd = square[:, 0, :]
        next_gain = sb("next_gain", [P, KD])
        ident, ones, ones_head = sb("ident", [P, P]), sb("ones", [P, P]), sb("ones_head", [P, P])
        par = sb("par", [P, NPAR])
        decay = sb("decay", [P, 2, KR])
        soft = sb("soft", [P, 4, KR])
        qg = sb("qg", [P, 1])
        carrier = sb("carrier", [1, HEADS * KS])
        mx, total, inv = sb("mx", [P, 2, KS]), sb("total", [P, 2, KS]), sb("inv", [P, 2, KS])

        def views(*parts):
            made = []
            with ExitStack() as scope:
                for n, (name, shape, dt) in enumerate(parts):
                    made.append(scope.enter_context(nc.sbuf_tensor(name, shape, dt)))
            return made

        R = KR * S
        act_hi, act_lo, gate, _ = views(("act_hi", [P, KF, S], F32R), ("act_lo", [P, KF, S], F32R),
                                        ("gate", [P, 2, S], F32), ("pad_f", [P, 2048], F32))
        u, u_hi, u_lo, r = views(("u", [P, KR, S], F32), ("u_hi", [P, KR, S], F32R), ("u_lo", [P, KR, S], F32R),
                                 ("r", [P, KR, S], F32))
        _, scan, y = views(("pad_a", [P, R], F32), ("scan", [P, KR, S], F32), ("y", [P, KR, S], F32))
        ya_hi, _, ya_lo = views(("ya_hi", [P, KR, S], F32R), ("pad_b", [P, 2 * R], F32), ("ya_lo", [P, KR, S], F32R))
        TRI = P * (KS * (KS + 1) // 2)
        q, v3, _, ya_out, pt, _, gb_out, p0, _, k, p1, _, v012 = views(
            ("q", [P, KD, S], F32), ("v3", [P, D], F32), ("pad_c", [P, R - KD * S - D], F32),
            ("ya_out", [P, KD, S], F32), ("pt", [P, TRI], F32), ("pad_d", [P, R - KD * S - TRI], F32),
            ("gb_out", [P, KD, S], F32), ("p0", [P, TRI], F32), ("pad_e", [P, R - KD * S - TRI], F32),
            ("k", [P, KD, S], F32), ("p1", [P, TRI], F32), ("pad_g", [P, R - KD * S - TRI], F32),
            ("v012", [P, 3, D], F32))
        m_hi, _, m_lo = views(("m_hi", [P, KD, S], F32R), ("pad_h", [P, 3 * R - KD * S], F32),
                              ("m_lo", [P, KD, S], F32R))
        x_tok, rel_t = views(("x_tok", [P, KS, D], F32), ("rel_t", [DEPTH * HEADS, RELROW], F32))
        y_tok, = views(("y_tok", [P, KS, D], F32))
        prob = [p0, p1]
        qk = [q, k]
        v = [v012[:, 0, :], v012[:, 1, :], v012[:, 2, :], v3[:, :]]

        ps = ctx.enter_context(nc.psum_tensor("ps", [P, 8, S], F32))

        hi_made, lo_made, chunk_begun = sem("hi_made"), sem("lo_made"), sem("chunk_begun")
        raw_loaded = [sem(f"raw_loaded{s}") for s in range(SLOTS)]
        for_act, for_dve = sem("for_act"), sem("for_dve")
        bank_read = [sem(f"bank_read{b}") for b in range(8)]
        silu_made = sem("silu_made")
        square_made, square_used, rstd_made = sem("square_made"), sem("square_used"), sem("rstd_made")
        to_split, split_hi, split_lo = sem("to_split"), sem("split_hi"), sem("split_lo")
        conv_begun, conv_step, gated, tanh_made = sem("conv_begun"), sem("conv_step"), sem("gated"), sem("tanh_made")
        logs_made, diff_made, drive_made = sem("logs_made"), sem("diff_made"), sem("drive_made")
        scan_step, soft_step, lam_exp, decay_made = sem("scan_step"), sem("soft_step"), sem("lam_exp"), sem("decay_made")
        gelu_made, qk_made, qk_rstd = sem("gelu_made"), sem("qk_made"), sem("qk_rstd")
        exp_made, prob_made, inv_made, band_masked = sem("exp_made"), sem("prob_made"), sem("inv_made"), sem("band_masked")
        q_placed = sem("q_placed")
        band_loaded = [sem(f"band_loaded{n}") for n in range(2)]
        par_loaded = sem("par_loaded")
        counted = {
            "hi_made": hi_made, "lo_made": lo_made, "chunk_begun": chunk_begun, "for_act": for_act, "silu_made": silu_made,
            "for_dve": for_dve, "square_made": square_made, "square_used": square_used, "rstd_made": rstd_made,
            "to_split": to_split, "split_hi": split_hi, "split_lo": split_lo, "conv_begun": conv_begun,
            "conv_step": conv_step, "gated": gated, "tanh_made": tanh_made, "logs_made": logs_made,
            "diff_made": diff_made, "drive_made": drive_made, "scan_step": scan_step, "soft_step": soft_step,
            "lam_exp": lam_exp, "decay_made": decay_made, "gelu_made": gelu_made, "qk_made": qk_made,
            "qk_rstd": qk_rstd, "exp_made": exp_made, "prob_made": prob_made, "inv_made": inv_made,
            "band_masked": band_masked, "q_placed": q_placed, "par_loaded": par_loaded,
            **{f"bank_read{b}": bank_read[b] for b in range(8)},
            **{f"raw_loaded{s}": raw_loaded[s] for s in range(SLOTS)},
            **{f"band_loaded{n}": band_loaded[n] for n in range(2)}}
        par_free, gain_loaded = sem("par_free"), sem("gain_loaded")
        x_loaded, rel_loaded, rel_padded, rel_stored, consts_made = (
            sem("x_loaded"), sem("rel_loaded"), sem("rel_padded"), sem("rel_stored"), sem("consts_made"))
        out_made, out_stored = sem("out_made"), sem("out_stored")

        STARTS = {"lo_made": SLOTS}

        def counts(**starts):
            return Counts(counted, {**STARTS, **starts})

        def mix_bank(n):
            return 2 + n % 6

        XR_T, RG_T, YR_T, G_T, UA_T, QK_T, V_T, UB_T, OUT_T = np.cumsum(
            [0, KR, 2 * KR, KR, 2 * KD, KD, 2 * KD, KD, KD]).tolist()

        block = ctx.enter_context(nc.Block())

        @block.sync
        def _(sp):
            C = counts(lo_made=0)
            place = [0]

            def load(src, shape):
                s = place[0] % SLOTS
                place[0] += 1
                sp.wait_ge(lo_made, C.next(lo_made))
                n = int(np.prod(shape))
                dst = raw[:, s, 0:n].rearrange("p (a b) -> p a b", a=shape[0]) if len(shape) == 2 else raw[:, s, 0:n]
                sp.dma_start(dst, src).then_inc(raw_loaded[s], 16)

            def rows(w, kt):
                return w.rearrange("l (k p) n -> p (l k) n", p=P)

            def pairs(w, kt, l, col, n_pairs, groups):
                v_ = rows(w, kt)
                for j in range(n_pairs):
                    for a, b in (groups[j] if isinstance(groups[0], list) else groups):
                        load(v_[:, bass.ds(l * kt + a, b - a), col + j * PAIR:col + (j + 1) * PAIR], (b - a, PAIR))

            def ffn(w_gate, w_up, w_down, l):
                g_, u_ = rows(w_gate, KD), rows(w_up, KD)
                with sp.Fori(0, TURNS) as i:
                    C.enter("turn", PER_TURN, i)
                    for w in (g_, u_):
                        for a, b in G8:
                            load(w[:, bass.ds(l * KD + a, 4), bass.ds(i * PAIR, PAIR)], (4, PAIR))
                    C.leave("turn", TURNS)
                pairs(w_down, KF, l, 0, KD // 2, G22)

            sp.dma_start(x_tok[:, :, :], x_in.rearrange("b (t p) d -> p (b t) d", p=P)).then_inc(x_loaded, 16)
            sp.dma_start(next_gain[:, :], first_gain).then_inc(gain_loaded, 16)
            sp.dma_start(rel_t[:, RELPAD:RELPAD + RELW], rel_rev).then_inc(rel_loaded, 16)

            with sp.Fori(0, DEPTH) as l:
                C.enter("layer", PER_LAYER, l)
                sp.wait_ge(par_free, l + 1)
                sp.dma_start(par[:, :].rearrange("p (a n) -> p a n", a=1),
                             params.rearrange("l p n -> p l n")[:, bass.ds(l, 1), :]).then_inc(par_loaded, 16)
                ffn(w_gate1, w_up1, w_down1, l)
                win = rows(w_in, KD)
                for base, band in ((XR0, False), (0, True), (YR0, False)):
                    if band:
                        bands = rg_band.rearrange("l p n -> p l n")
                        for c in range(RG_CHUNKS):
                            n = min(CW, len(BANDS) * P - c * CW)
                            load(bands[:, bass.ds(l, 1), c * CW:c * CW + n], (1, n))
                    else:
                        pairs(w_in, KD, l, base, KR // 2, G8)
                        load(win[:, bass.ds(l * KD, KD), base + (KR - 1) * P:base + KR * P], (KD, P))
                pairs(w_in, KD, l, G0, KD, G8)
                pairs(w_up_a, KR, l, 0, KD // 2, UP_A)
                pairs(w_in, KD, l, Q0, KD, G8)
                for half in range(2):
                    for a in range(0, KD, 2):
                        load(win[:, bass.ds(l * KD + a, 2), V0 + half * S:V0 + (half + 1) * S], (2, S))
                pairs(w_up_b, KD, l, 0, 2, G8)
                sp.wait_ge(band_masked, C.next(band_masked))
                sp.wait_ge(rel_stored, 32)
                for head in range(HEADS):
                    if head >= 2:
                        sp.wait_ge(exp_made, C.next(exp_made, KS))
                    band = rel_band[:, :, :].rearrange("h p n -> p h n")[:, bass.ds(l * HEADS + head, 1), :]
                    for p_, w_ in ((0, S - CHUNK), (CHUNK, S)):
                        sp.dma_start(tmp[p_:p_ + CHUNK, head % 2, 0:w_].rearrange("p (a n) -> p a n", a=1),
                                     band[p_:p_ + CHUNK, :, 0:w_]).then_inc(band_loaded[head % 2], 16)
                C.step(exp_made, 2 * KS)
                v_ = rows(w_up_b, KD)
                for j in range(2, KD // 2):
                    for a, b in G8:
                        load(v_[:, bass.ds(l * KD + a, b - a), j * PAIR:(j + 1) * PAIR], (b - a, PAIR))
                pairs(w_out, KD, l, 0, KD // 2, G8)
                ffn(w_gate2, w_up2, w_down2, l)
                C.leave("layer", DEPTH)
            for _ in range(AHEAD):
                load(rows(w_up_b, KD)[:, 0:4, 0:PAIR], (4, PAIR))
            sp.wait_ge(out_made, 2 * KS)
            sp.dma_start(out.rearrange("b (t p) d -> p (b t) d", p=P), y_tok[:, :, :]).then_inc(out_stored, 16)
            sp.wait_ge(out_stored, 16)

        @block.gpsimd
        def _(pool):
            C = counts()
            nc.gpsimd.memset(soft[:, 0, :], 0.0).then_inc(chunk_begun, AHEAD)
            nc.gpsimd.memset(soft[:, 1, :], 0.0).then_inc(square_used, 2)
            nc.gpsimd.memset(soft[:, 2, :], 0.0).then_inc(par_free, 1)
            nc.gpsimd.memset(ident[:, :], 0.0).then_inc(consts_made, 1)
            nc.gpsimd.memset(ones[:, :], 1.0).then_inc(lo_made, SLOTS)
            nc.gpsimd.memset(ones_head[:, :], 0.0).then_inc(consts_made, 1)
            pool.wait_ge(consts_made, 2)
            nc.gpsimd.affine_select(out=ident[:, :], in_=ident[:, :], compare_op=ALU.not_equal, fill=1.0, base=0,
                                    pattern=[[-1, P]], channel_multiplier=1).then_inc(consts_made, 1)
            nc.gpsimd.memset(ones_head[0:HD, 0:HD], 1.0).then_inc(consts_made, 1)
            pool.wait_ge(consts_made, 4)
            nc.gpsimd.memset(ones_head[HD:P, HD:P], 1.0).then_inc(consts_made, 1)
            pool.wait_ge(consts_made, 5)

            def lo(c, s):
                pool.wait_ge(hi_made, c + 1)
                nc.gpsimd.tensor_tensor(wlo[:, s, :], raw[:, s, :], whi[:, s, :].bitcast(F32),
                                        ALU.subtract).then_inc(lo_made, 1)

            for c in range(AHEAD):
                lo(c, c)
            with pool.Fori(0, DEPTH) as l:
                C.enter("layer", PER_LAYER, l)
                with pool.Fori(0, BEFORE_ATTENTION // SLOTS) as n:
                    for s in range(SLOTS):
                        lo(l * CHUNKS + n * SLOTS + (AHEAD + s), (AHEAD + s) % SLOTS)
                pool.wait_ge(qk_made, C.next(qk_made, 2 * KD))
                for head in range(HEADS):
                    if head >= 2:
                        pool.wait_ge(prob_made, C.next(prob_made, KS))
                    if head:
                        pool.wait_ge(q_placed, C.now(q_placed))
                    p_ = head % 2 * HD
                    zeros = ones_head[p_:p_ + HD, HD - p_:HD - p_ + 1].to_broadcast([HD, S])
                    nc.gpsimd.tensor_tensor(square[p_:p_ + HD, head % 2, :], q[p_:p_ + HD, head // 2, :], zeros,
                                            ALU.add).then_inc(q_placed, C.made(q_placed))
                    if head < 2:
                        nc.gpsimd.tensor_tensor(square[p_:p_ + HD, 1 - head % 2, :], zeros, zeros, ALU.add
                                                ).then_inc(q_placed, C.made(q_placed))
                C.step(prob_made, 2 * KS)
                with pool.Fori(0, (CHUNKS - BEFORE_ATTENTION) // SLOTS) as n:
                    for s in range(SLOTS):
                        lo(l * CHUNKS + n * SLOTS + (BEFORE_ATTENTION + AHEAD + s), (AHEAD + s) % SLOTS)
                C.leave("layer", DEPTH)

        @block.scalar
        def _(act):
            C = counts()
            place = [0]

            def ring(n=1):
                for _ in range(n):
                    s = place[0] % SLOTS
                    place[0] += 1
                    act.wait_ge(chunk_begun, C.next(chunk_begun))
                    act.wait_ge(raw_loaded[s], C.next(raw_loaded[s], 16))
                    nc.scalar.activation(whi[:, s, :], raw[:, s, :], ACT.Copy).then_inc(hi_made, C.made(hi_made))

            def col(name, j=0):
                return par[:, PAR[name] + j:PAR[name] + j + 1]

            def read(b, dst, func, **how):
                act.wait_ge(for_act, C.next(for_act))
                nc.scalar.activation(dst, ps[:, b, :], func, **how).then_inc(bank_read[b], C.made(bank_read[b]))

            def hi_of(dst, src):
                act.wait_ge(to_split, C.next(to_split))
                nc.scalar.activation(dst, src, ACT.Copy).then_inc(split_hi, C.made(split_hi))

            def squared(t, src):
                act.wait_ge(square_used, C.next(square_used))
                nc.scalar.activation(square[:, t % 2, :], src, ACT.Square).then_inc(square_made, C.made(square_made))

            def summed(ahead):
                C.step(square_used, ahead)
                act.wait_ge(square_used, C.now(square_used))
                C.step(square_used, -ahead)

            def rstd_from(b):
                act.preload_act_table_set("natural_log_exp_and_others")
                summed(2)
                nc.scalar.activation(rstd, ps[:, b, :], ACT.Ln, scale=1.0 / D, bias=EPS
                                     ).then_inc(bank_read[b], C.made(bank_read[b]))
                act.wait_ge(bank_read[b], C.now(bank_read[b]))
                nc.scalar.activation(rstd, rstd, ACT.Exp, scale=-0.5).then_inc(rstd_made, C.made(rstd_made))

            def renewed(t, b, to_ffn):
                C.step(bank_read[b])
                if to_ffn:
                    hi_of(h_hi[:, t, :], tmp[:, t % 2, :])
                else:
                    act.wait_ge(bank_read[b], C.now(bank_read[b]))
                squared(t, x[:, t, :])

            def ffn(to_ffn):
                with act.Fori(0, TURNS) as i:
                    C.enter("turn", PER_TURN, i)
                    ring(2)
                    for m in range(2):
                        C.step(bank_read[m])
                        act.wait_ge(bank_read[m], C.now(bank_read[m]))
                        nc.scalar.activation(gate[:, m, :], gate[:, m, :], ACT.Silu
                                             ).then_inc(silu_made, C.made(silu_made))
                    ring(2)
                    for m in range(2):
                        C.step(bank_read[2 + m])
                        hi_of(act_hi[:, :, :].rearrange("p k s -> p (k s)")[:, bass.ds((i * 2 + m) * S, S)],
                              tmp[:, m, :])
                    C.leave("turn", TURNS)
                for j in range(KD // 2):
                    ring(len(G22))
                    for t in (2 * j, 2 * j + 1):
                        renewed(t, 4 + t % 4, to_ffn)

            act.wait_ge(rel_padded, 1)
            act.dma_start(rel_rows[:, :], rel_t[:, :]).then_inc(rel_stored, 16)
            act.wait_ge(rel_stored, 16)
            ring(AHEAD)
            for t in range(KD):
                renewed(t, t, True)
            act.dma_start(rel_band[:, :, :], bass.AP(rel_rows, P - 1, [[RELROW, DEPTH * HEADS], [-1, P], [1, S]])
                          ).then_inc(rel_stored, 16)

            with act.Fori(0, DEPTH) as l:
                C.enter("layer", PER_LAYER, l)
                C.step(par_loaded, 16)
                rstd_from(4)
                C.step(soft_step, 2)
                act.wait_ge(soft_step, C.now(soft_step))
                nc.scalar.activation(soft[:, 1, :], soft[:, 1, :], ACT.Exp, scale=-1.0
                    ).then_inc(lam_exp, C.made(lam_exp))
                C.step(soft_step, 16)
                ffn(False)
                rstd_from(0)
                for t in range(KD):
                    hi_of(h_hi[:, t, :], tmp[:, t % 2, :])

                def conv_init(t):
                    act.wait_ge(for_act, C.next(for_act))
                    nc.scalar.activation(
                        u[:, t, :], ps[:, mix_bank(XR_T + t), :], ACT.Identity,
                        scale=col("conv_w", (CONV - 1) * KR + t), bias=col("conv_b", t)
                            ).then_inc(conv_begun, C.made(conv_begun))
                    C.step(bank_read[mix_bank(XR_T + t)])

                def conv_hi(t):
                    act.wait_ge(bank_read[mix_bank(XR_T + t)], C.now(bank_read[mix_bank(XR_T + t)]))
                    nc.scalar.activation(u_hi[:, t, :], u[:, t, :], ACT.Copy).then_inc(split_hi, C.made(split_hi))

                for t in range(0, KR, 2):
                    ring()
                    if t:
                        conv_hi(t - 2)
                        conv_hi(t - 1)
                    if t + 1 < KR:
                        ring()
                        conv_init(t)
                        conv_init(t + 1)
                conv_init(KR - 1)
                conv_hi(KR - 1)

                blocks = chunks = 0
                for m in range(KR):
                    for g in range(2):
                        blocks += sum(b[:2] == (m, g) for b in BANDS)
                        while chunks * BPC < blocks:
                            ring()
                            chunks += 1
                        if g and m >= 2:
                            act.wait_ge(gated, C.next(gated))
                        read(mix_bank(RG_T + 2 * m + g), gate[:, m % 2, :] if g else r[:, m, :], ACT.Sigmoid,
                             bias=col("b_x" if g else "b_a", m))
                act.wait_ge(bank_read[mix_bank(RG_T + 2 * KR - 1)], C.now(bank_read[mix_bank(RG_T + 2 * KR - 1)]))
                act.wait_ge(decay_made, C.next(decay_made))

                for m in range(KR):
                    nc.scalar.activation(scan[:, m, :], r[:, m, :], ACT.Tanh,
                                                               scale=decay[:, 0, m:m + 1]
                                                                   ).then_inc(tanh_made, C.made(tanh_made))
                    if m in (KR // 2, KR - 1):
                        ring()
                act.preload_act_table_set("natural_log_exp_and_others")
                act.wait_ge(tanh_made, C.now(tanh_made))
                for m in range(KR + 2):
                    if m >= 2:
                        act.wait_ge(diff_made, C.next(diff_made))
                        nc.scalar.activation(scan[:, m - 2, :], scan[:, m - 2, :], ACT.Exp,
                                                                    scale=0.5, bias=HALF_LN2
                                                                        ).then_inc(drive_made, C.made(drive_made))
                    if m < KR:
                        if m == 0:
                            act.wait_ge(gated, C.next(gated, 2))
                        nc.scalar.activation(gate[:, m % 2, :], scan[:, m, :], ACT.Ln, bias=1.0)
                        nc.scalar.activation(scan[:, m, :], scan[:, m, :], ACT.Ln, bias=TINY
                            ).then_inc(logs_made, C.made(logs_made))
                        nc.scalar.activation(r[:, m, :], r[:, m, :], ACT.Exp, scale=decay[:, 1, m:m + 1])
                    if m % 2 and m <= KR:
                        ring()

                ring()
                for t in range(KR + 2):
                    if t < KR:
                        b = mix_bank(YR_T + t)
                        C.step(bank_read[b])
                        act.wait_ge(bank_read[b], C.now(bank_read[b]))
                        nc.scalar.activation(y[:, t, :], y[:, t, :], ACT.Gelu_apprx_tanh
                                             ).then_inc(gelu_made, C.made(gelu_made))
                    if t >= 2:
                        hi_of(ya_hi[:, t - 2, :], tmp[:, t % 2, :])
                    if t in (2, 5, 8, 10):
                        ring()
                for t in range(2 * KD):
                    if t % 2 == 0 and t:
                        ring(2)
                    read(mix_bank(G_T + t), ya_out[:, t, :] if t < KD else gb_out[:, t - KD, :], ACT.Sigmoid,
                         bias=col("gate", t))
                for j in range(KD // 2):
                    ring(len(UP_A[j]))
                for t in range(KD):
                    C.step(bank_read[mix_bank(UA_T + t)])

                act.preload_act_table_set("natural_log_exp_and_others")

                def head_rstd(t, ahead):
                    if t >= 2:
                        act.wait_ge(qk_made, C.next(qk_made))
                    summed(ahead)
                    nc.scalar.activation(gate[:, t % 2, :], ps[:, t % 2, :], ACT.Ln,
                                                              scale=1.0 / HD, bias=EPS
                            ).then_inc(bank_read[t % 2], C.made(bank_read[t % 2]))
                    act.wait_ge(bank_read[t % 2], C.now(bank_read[t % 2]))
                    nc.scalar.activation(gate[:, t % 2, :], gate[:, t % 2, :], ACT.Exp,
                                                             scale=-0.5).then_inc(qk_rstd, C.made(qk_rstd))

                for t in range(0, 2 * KD, 2):
                    ring(2)
                    for n in (t, t + 1):
                        b = mix_bank(QK_T + n)
                        act.wait_ge(for_act, C.next(for_act))
                        squared(n, ps[:, b, :])
                        nc.scalar.activation(qk[n // KD][:, n % KD, :], ps[:, b, :], ACT.Copy
                            ).then_inc(bank_read[b], C.made(bank_read[b]))
                    if t:
                        head_rstd(t - 2, -1)
                        head_rstd(t - 1, 0)
                head_rstd(2 * KD - 2, 1)
                head_rstd(2 * KD - 1, 2)
                C.step(qk_made, 2)

                ring(8)
                for n in range(2 * KS):
                    C.step(bank_read[mix_bank(V_T + n)])

                def exps(head):
                    for i in range(KS):
                        C.step(bank_read[i])
                        act.wait_ge(bank_read[i], C.now(bank_read[i]))
                        part = prob[head % 2][:, tri(i):tri(i + 1)]
                        nc.scalar.activation(part, part, ACT.Exp, scale=-1.0,
                                                                  bias=mx[:, head % 2, i:i + 1],
                                                                  accum_out=total[:, head % 2, i:i + 1]
                                                                      ).then_inc(exp_made, C.made(exp_made))

                exps(0)
                exps(1)
                for head in range(HEADS):
                    for b, at, width, _ in TURNED:
                        act.wait_ge(for_act, C.next(for_act))
                        nc.scalar.activation(pt[:, at:at + width], ps[:, b, 0:width], ACT.Copy
                                             ).then_inc(bank_read[b], C.made(bank_read[b]))
                    if head + 2 < HEADS:
                        exps(head + 2)
                    if head % 2:
                        act.wait_ge(for_act, C.next(for_act))
                        nc.scalar.activation(h_hi[:, head // 2, :], ps[:, 6, :], ACT.Copy
                                             ).then_inc(split_hi, C.made(split_hi))
                        C.step(bank_read[6])

                for t in range(KD):
                    if t % 2 == 0:
                        ring(2)
                    C.step(bank_read[mix_bank(UB_T + t)])
                    hi_of(m_hi[:, t, :], tmp[:, t % 2, :])
                for t in range(KD):
                    if t % 2 == 0:
                        ring(2)
                    renewed(t, mix_bank(OUT_T + t), True)
                rstd_from(4)
                ffn(True)
                C.leave("layer", DEPTH)

            for t in range(KS):
                act.wait_ge(for_act, C.next(for_act))
                nc.scalar.activation(y_tok[:, t, 0:S], ps[:, 2 * t, :], ACT.Copy).then_inc(out_made, 1)

        @block.vector
        def _(dve):
            C = counts(square_used=2)

            def col(name, j=0):
                return par[:, PAR[name] + j:PAR[name] + j + 1]

            def lo_of(dst, src, hi):
                dve.wait_ge(split_hi, C.next(split_hi))
                nc.vector.tensor_tensor(dst, src, hi.bitcast(F32), ALU.subtract).then_inc(split_lo, C.made(split_lo))

            def added(t):
                dve.wait_ge(square_made, C.next(square_made, 2 if t == 1 else 1))
                if t > 1:
                    dve.wait_ge(square_used, C.now(square_used))
                nc.vector.tensor_tensor(square[:, t % 2, :], square[:, t % 2, :], square[:, (t + 1) % 2, :],
                                        ALU.add).then_inc(square_used, C.made(square_used))

            def squares_behind(t):
                if 2 <= t < KD - 1:
                    added(t - 1)
                if t == KD - 2:
                    added(t)
                if t == KD - 1:
                    C.step(square_made)
                    C.step(square_used, 2)

            def renewed(t, gain, first=False):
                if t >= 2 or not first:
                    dve.wait_ge(split_lo, C.now(split_lo))
                nc.vector.tensor_scalar(tmp[:, t % 2, :], x[:, t, :], gain, None, ALU.mult
                                        ).then_inc(to_split, C.made(to_split))
                if t >= 1:
                    lo_of(h_lo[:, t - 1, :], tmp[:, (t - 1) % 2, :], h_hi[:, t - 1, :])
                if t >= 2:
                    added(t - 1)
                if t == KD - 1:
                    lo_of(h_lo[:, t, :], tmp[:, t % 2, :], h_hi[:, t, :])
                    C.step(square_made)
                    C.step(square_used, 2)

            def norm(name):
                C.step(bank_read[0])
                dve.wait_ge(rstd_made, C.next(rstd_made))

                def scaled(t):
                    nc.vector.scalar_tensor_tensor(
                        tmp[:, t % 2, :], x[:, t, :], col(name, t), rstd, ALU.mult, ALU.mult
                            ).then_inc(to_split, C.made(to_split))

                scaled(0)
                scaled(1)
                for t in range(KD):
                    lo_of(h_lo[:, t, :], tmp[:, t % 2, :], h_hi[:, t, :])
                    if t + 2 < KD:
                        dve.wait_ge(split_lo, C.now(split_lo))
                        scaled(t + 2)

            def ffn(to_ffn):
                with dve.Fori(0, TURNS) as i:
                    C.enter("turn", PER_TURN, i)
                    for m in range(2):
                        dve.wait_ge(for_dve, C.next(for_dve))
                        nc.vector.tensor_tensor(gate[:, m, :], ps[:, m, :], rstd, ALU.mult
                                                ).then_inc(bank_read[m], C.made(bank_read[m]))
                    for m in range(2):
                        dve.wait_ge(split_lo, C.now(split_lo, 1 - m))
                        dve.wait_ge(for_dve, C.next(for_dve))
                        nc.vector.tensor_tensor(tmp[:, m, :], ps[:, 2 + m, :], rstd, ALU.mult
                                                ).then_inc(bank_read[2 + m], C.made(bank_read[2 + m]))
                    for m in range(2):
                        dve.wait_ge(silu_made, C.next(silu_made))
                        dve.wait_ge(bank_read[2 + m], C.now(bank_read[2 + m]))
                        nc.vector.tensor_tensor(tmp[:, m, :], tmp[:, m, :], gate[:, m, :], ALU.mult
                                                ).then_inc(to_split, C.made(to_split))
                    for m in range(2):
                        at = bass.ds((i * 2 + m) * S, S)
                        lo_of(act_lo[:, :, :].rearrange("p k s -> p (k s)")[:, at], tmp[:, m, :],
                              act_hi[:, :, :].rearrange("p k s -> p (k s)")[:, at])
                    C.leave("turn", TURNS)
                for t in range(KD):
                    dve.wait_ge(for_dve, C.next(for_dve))
                    nc.vector.scalar_tensor_tensor(
                        x[:, t, :], ps[:, 4 + t % 4, :], 0.5, x[:, t, :], ALU.mult, ALU.add
                        ).then_inc(bank_read[4 + t % 4], C.made(bank_read[4 + t % 4]))
                    if to_ffn:
                        dve.wait_ge(bank_read[4 + t % 4], C.now(bank_read[4 + t % 4]))
                        renewed(t, next_gain[:, t:t + 1])
                    else:
                        squares_behind(t)

            dve.wait_ge(rel_loaded, 16)
            nc.vector.tensor_copy(rel_t[:, 0:RELPAD],
                                  rel_t[:, RELPAD:RELPAD + 1].to_broadcast([DEPTH * HEADS, RELPAD])
                                  ).then_inc(rel_padded, 1)
            dve.wait_ge(gain_loaded, 16)
            for t in range(KD):
                dve.wait_ge(for_dve, C.next(for_dve))
                nc.vector.tensor_copy(x[:, t, :], ps[:, t, :]).then_inc(bank_read[t], C.made(bank_read[t]))
                dve.wait_ge(bank_read[t], C.now(bank_read[t]))
                renewed(t, next_gain[:, t:t + 1], True)

            with dve.Fori(0, DEPTH) as l:
                C.enter("layer", PER_LAYER, l)
                dve.wait_ge(par_loaded, C.next(par_loaded, 16))
                lam = par[:, PAR["lam"]:PAR["lam"] + KR]
                neg, z, c, e = (soft[:, n, :] for n in range(4))
                nc.vector.tensor_scalar(neg, lam, -1.0, None, ALU.mult).then_inc(soft_step, C.made(soft_step))
                dve.wait_ge(soft_step, C.now(soft_step))
                nc.vector.tensor_tensor(z, neg, lam, ALU.max).then_inc(soft_step, C.made(soft_step))
                C.step(bank_read[4])
                dve.wait_ge(rstd_made, C.next(rstd_made))
                dve.wait_ge(lam_exp, C.next(lam_exp))
                nc.vector.tensor_scalar(c, z, 2.0, None, ALU.add).then_inc(soft_step, C.made(soft_step))
                dve.wait_ge(soft_step, C.now(soft_step))
                nc.vector.reciprocal(c, c).then_inc(soft_step, C.made(soft_step))
                dve.wait_ge(soft_step, C.now(soft_step))
                nc.vector.tensor_tensor(z, z, c, ALU.mult).then_inc(soft_step, C.made(soft_step))
                dve.wait_ge(soft_step, C.now(soft_step))
                nc.vector.tensor_tensor(c, z, z, ALU.mult).then_inc(soft_step, C.made(soft_step))
                dve.wait_ge(soft_step, C.now(soft_step))
                nc.vector.tensor_scalar(e, c, 1.0 / 17, None, ALU.mult).then_inc(soft_step, C.made(soft_step))
                dve.wait_ge(soft_step, C.now(soft_step))
                for n in range(15, 1, -2):
                    nc.vector.scalar_tensor_tensor(e, e, 1.0 / n, c, ALU.add, ALU.mult
                        ).then_inc(soft_step, C.made(soft_step))
                    dve.wait_ge(soft_step, C.now(soft_step))
                nc.vector.scalar_tensor_tensor(e, e, 1.0, z, ALU.add, ALU.mult).then_inc(soft_step, C.made(soft_step))
                dve.wait_ge(soft_step, C.now(soft_step))
                nc.vector.tensor_scalar(neg, neg, 0.0, LRU_C, ALU.max, ALU.mult).then_inc(soft_step, C.made(soft_step))
                dve.wait_ge(soft_step, C.now(soft_step))
                nc.vector.scalar_tensor_tensor(decay[:, 0, :], e, 2 * LRU_C, neg, ALU.mult,
                                                                  ALU.add).then_inc(soft_step, C.made(soft_step))
                dve.wait_ge(soft_step, C.now(soft_step))
                nc.vector.tensor_scalar(decay[:, 1, :], decay[:, 0, :], -1.0, None, ALU.mult
                    ).then_inc(soft_step, C.made(soft_step))
                dve.wait_ge(soft_step, C.now(soft_step))
                nc.vector.tensor_scalar(qg[:, :], col("q_gain"), HD ** -0.5, None, ALU.mult
                    ).then_inc(decay_made, C.made(decay_made))
                ffn(False)
                norm("mix")

                def conv(t):
                    b = mix_bank(XR_T + t)
                    dve.wait_ge(conv_begun, C.next(conv_begun))
                    for back in range(1, CONV):
                        ins = nc.vector.scalar_tensor_tensor(
                            u[:, t, back:S], ps[:, b, 0:S - back], col("conv_w", (CONV - 1 - back) * KR + t),
                            u[:, t, back:S], ALU.mult, ALU.add)
                        if back < CONV - 1:
                            ins.then_inc(conv_step, C.made(conv_step))
                            dve.wait_ge(conv_step, C.now(conv_step))
                        else:
                            ins.then_inc(bank_read[b], C.made(bank_read[b]))

                for t in range(0, KR, 2):
                    both = range(t, min(t + 2, KR))
                    for n in both:
                        conv(n)
                    for n in both:
                        lo_of(u_lo[:, n, :], u[:, n, :], u_hi[:, n, :])
                for m in range(KR):
                    C.step(bank_read[mix_bank(RG_T + 2 * m)])
                    C.step(bank_read[mix_bank(RG_T + 2 * m + 1)])
                    dve.wait_ge(bank_read[mix_bank(RG_T + 2 * m + 1)], C.now(bank_read[mix_bank(RG_T + 2 * m + 1)]))
                    nc.vector.tensor_tensor(u[:, m, :], u[:, m, :], gate[:, m % 2, :], ALU.mult
                        ).then_inc(gated, C.made(gated))
                def yr_out(t):
                    dve.wait_ge(for_dve, C.next(for_dve))
                    nc.vector.tensor_copy(y[:, t, :], ps[:, mix_bank(YR_T + t), :]
                                          ).then_inc(bank_read[mix_bank(YR_T + t)],
                                                     C.made(bank_read[mix_bank(YR_T + t)]))

                for m in range(KR + 3):
                    if m in (3, 7, 11):
                        yr_out((m - 3) // 2)
                        yr_out((m - 3) // 2 + 1)
                    if m < KR:
                        dve.wait_ge(logs_made, C.next(logs_made))
                        nc.vector.tensor_tensor(scan[:, m, :], scan[:, m, :],
                                                                      gate[:, m % 2, :], ALU.subtract
                                                                          ).then_inc(diff_made, C.made(diff_made))
                    if m >= 3:
                        n = m - 3
                        dve.wait_ge(drive_made, C.next(drive_made))
                        nc.vector.tensor_tensor(scan[:, n, :], scan[:, n, :], u[:, n, :],
                                                                   ALU.mult).then_inc(scan_step, C.made(scan_step))
                        dve.wait_ge(scan_step, C.now(scan_step))
                        nc.vector.tensor_tensor_scan(scan[:, n, :], r[:, n, :], scan[:, n, :],
                                                                           0.0, ALU.mult, ALU.add
                                                                               ).then_inc(scan_step, C.made(scan_step))
                dve.wait_ge(scan_step, C.now(scan_step))

                def gated_h(t):
                    dve.wait_ge(gelu_made, C.next(gelu_made))
                    nc.vector.tensor_tensor(tmp[:, t % 2, :], y[:, t, :], scan[:, t, :],
                                            ALU.mult).then_inc(to_split, C.made(to_split))

                yr_out(6)
                yr_out(7)
                gated_h(0)
                gated_h(1)
                for t in range(KR):
                    if t == 3:
                        yr_out(8)
                        yr_out(9)
                    if t == 6:
                        yr_out(10)
                    lo_of(ya_lo[:, t, :], tmp[:, t % 2, :], ya_hi[:, t, :])
                    if t + 2 < KR:
                        dve.wait_ge(split_lo, C.now(split_lo))
                        gated_h(t + 2)
                dve.wait_ge(split_lo, C.now(split_lo))
                nc.vector.memset(tmp[0:CHUNK, 0, S - CHUNK:S], -1e30)
                nc.vector.memset(tmp[0:CHUNK, 1, S - CHUNK:S], -1e30).then_inc(band_masked, C.made(band_masked))
                for t in range(2 * KD):
                    C.step(bank_read[mix_bank(G_T + t)])
                    if t == KD - 1:
                        dve.wait_ge(bank_read[mix_bank(G_T + t)], C.now(bank_read[mix_bank(G_T + t)]))
                for t in range(KD):
                    b = mix_bank(UA_T + t)
                    dve.wait_ge(for_dve, C.next(for_dve))
                    nc.vector.tensor_tensor(ya_out[:, t, :], ps[:, b, :], ya_out[:, t, :], ALU.mult
                                            ).then_inc(bank_read[b], C.made(bank_read[b]))

                C.step(square_made, 2 * KD)
                C.step(square_used, 2 * KD)

                def qk_scaled(t):
                    C.step(bank_read[t % 2])
                    dve.wait_ge(qk_rstd, C.next(qk_rstd))
                    part = qk[t // KD][:, t % KD, :]
                    nc.vector.scalar_tensor_tensor(
                        part, part, col("k_gain") if t >= KD else qg[:, :], gate[:, t % 2, :], ALU.mult, ALU.mult
                            ).then_inc(qk_made, C.made(qk_made))

                for t in range(2 * KD):
                    C.step(bank_read[mix_bank(QK_T + t)])
                    if t % 2 and t > 1:
                        qk_scaled(t - 3)
                        qk_scaled(t - 2)
                qk_scaled(2 * KD - 2)
                qk_scaled(2 * KD - 1)
                dve.wait_ge(qk_made, C.now(qk_made))
                for half in range(2):
                    for t in range(KS):
                        b = mix_bank(V_T + half * KS + t)
                        dve.wait_ge(for_dve, C.next(for_dve))
                        nc.vector.tensor_copy(v[t][:, half * S:(half + 1) * S], ps[:, b, :]
                            ).then_inc(bank_read[b], C.made(bank_read[b]))

                def biased(head):
                    dve.wait_ge(band_loaded[head % 2], C.next(band_loaded[head % 2], 32))
                    for i in range(KS):
                        dve.wait_ge(for_dve, C.next(for_dve))
                        nc.vector.memset(carrier[0:1, head * KS + i:head * KS + i + 1], 0.0)
                        nc.vector.tensor_tensor_reduce(
                            prob[head % 2][:, tri(i):tri(i + 1)], ps[:, i, 0:(i + 1) * P],
                            tmp[:, head % 2, S - (i + 1) * P:S], -1.0, 3e38, ALU.add, ALU.min,
                            mx[:, head % 2, i:i + 1]).then_inc(bank_read[i], C.made(bank_read[i]))

                def normalised(head):
                    e = head % 2
                    dve.wait_ge(exp_made, C.next(exp_made, KS))
                    nc.vector.reciprocal(inv[:, e, :], total[:, e, :]).then_inc(inv_made, C.made(inv_made))
                    dve.wait_ge(inv_made, C.now(inv_made))
                    for i in range(KS):
                        part = prob[e][:, tri(i):tri(i + 1)]
                        nc.vector.tensor_scalar(part, part, inv[:, e, i:i + 1], None, ALU.mult
                                                ).then_inc(prob_made, C.made(prob_made))

                biased(0)
                biased(1)
                normalised(0)
                for head in range(HEADS):
                    if head + 1 < HEADS:
                        normalised(head + 1)
                    if head + 2 < HEADS:
                        biased(head + 2)
                    for b, *_ in TURNED:
                        C.step(bank_read[b])
                    if head % 2:
                        t = head // 2
                        dve.wait_ge(split_hi, C.next(split_hi))
                        nc.vector.tensor_tensor(h_lo[:, t, :], ps[:, 6, :], h_hi[:, t, :].bitcast(F32), ALU.subtract
                                                ).then_inc(bank_read[6], C.made(bank_read[6]))

                def merged(t):
                    b = mix_bank(UB_T + t)
                    dve.wait_ge(for_dve, C.next(for_dve))
                    nc.vector.tensor_tensor(tmp[:, t % 2, :], ps[:, b, :], gb_out[:, t, :],
                                                             ALU.mult).then_inc(bank_read[b], C.made(bank_read[b]))
                    dve.wait_ge(bank_read[b], C.now(bank_read[b]))
                    nc.vector.tensor_tensor(tmp[:, t % 2, :], tmp[:, t % 2, :],
                                                                 ya_out[:, t, :], ALU.add
                                                                     ).then_inc(to_split, C.made(to_split))

                merged(0)
                merged(1)
                for t in range(KD):
                    lo_of(m_lo[:, t, :], tmp[:, t % 2, :], m_hi[:, t, :])
                    if t + 2 < KD:
                        dve.wait_ge(split_lo, C.now(split_lo))
                        merged(t + 2)
                for t in range(KD):
                    b = mix_bank(OUT_T + t)
                    dve.wait_ge(for_dve, C.next(for_dve))
                    nc.vector.tensor_tensor(x[:, t, :], ps[:, b, :], x[:, t, :], ALU.add
                                            ).then_inc(bank_read[b], C.made(bank_read[b]))
                    dve.wait_ge(bank_read[b], C.now(bank_read[b]))
                    renewed(t, col("ffn2", t))
                C.step(bank_read[4])
                dve.wait_ge(rstd_made, C.next(rstd_made))
                nc.vector.tensor_copy(next_gain[:, :], par[:, PAR["ffn1_next"]:PAR["ffn1_next"] + KD]
                                      ).then_inc(par_free, 1)
                ffn(True)
                C.leave("layer", DEPTH)

            for t in range(KS):
                dve.wait_ge(for_dve, C.next(for_dve))
                nc.vector.tensor_copy(y_tok[:, t, S:D], ps[:, 2 * t + 1, :]).then_inc(out_made, 1)

        @block.tensor
        def _(pe):
            C = counts()
            place = [0]
            begun = [True]

            def chunk():
                s = place[0] % SLOTS
                place[0] += 1
                pe.wait_ge(lo_made, C.next(lo_made))
                begun[0] = False
                return s

            def product(b, w_hi, w_lo, x_hi, x_lo, start, stop):
                ins = pe.matmul(ps[:, b, :], w_hi, x_lo, start=start, stop=False)
                if not begun[0]:
                    ins.then_inc(chunk_begun, C.made(chunk_begun))
                    begun[0] = True
                pe.matmul(ps[:, b, :], w_hi, x_hi, start=False, stop=False)
                return pe.matmul(ps[:, b, :], w_lo, x_hi, start=False, stop=stop)

            def columns(s, at, m):
                return whi[:, s, at + m * P:at + (m + 1) * P], wlo[:, s, at + m * P:at + (m + 1) * P]

            def pair(groups, kt, banks, hi, lo, ready, wait, behind=None):
                for g, (a, z) in enumerate(groups):
                    s = chunk()
                    for m, b in enumerate(banks):
                        if g == 0:
                            pe.wait_ge(bank_read[b], C.now(bank_read[b]))
                        for kk in range(a, z):
                            if wait and m == 0:
                                pe.wait_ge(split_lo, C.next(split_lo))
                            ins = product(b, *columns(s, (kk - a) * PAIR, m), hi[:, kk, :], lo[:, kk, :],
                                          kk == 0, kk == kt - 1)
                        if g == len(groups) - 1:
                            ins.then_inc(ready, C.made(ready))
                            C.step(bank_read[b])
                    if behind:
                        behind(g)

            def single(b, hi, lo, ready):
                s = chunk()
                pe.wait_ge(bank_read[b], C.now(bank_read[b]))
                for kk in range(KD):
                    ins = product(b, *columns(s, kk * P, 0), hi[:, kk, :], lo[:, kk, :], kk == 0, kk == KD - 1)
                ins.then_inc(ready, C.made(ready))
                C.step(bank_read[b])

            def summed(b):
                pe.wait_ge(square_made, C.next(square_made, KD))
                pe.wait_ge(bank_read[b], C.now(bank_read[b]))
                for n in range(2):
                    pe.matmul(ps[:, b, :], ones[:, :], square[:, n, :], start=n == 0, stop=n == 1
                              ).then_inc(square_used, 1)
                C.step(bank_read[b])

            def ffn():
                pair(G8, KD, (0, 1), h_hi, h_lo, for_dve, True, lambda g: g == 0 and summed(4))
                pair(G8, KD, (2, 3), h_hi, h_lo, for_dve, False)
                with pe.Fori(1, TURNS) as i:
                    C.enter("turn", PER_TURN, i, 1)
                    pair(G8, KD, (0, 1), h_hi, h_lo, for_dve, False)
                    pair(G8, KD, (2, 3), h_hi, h_lo, for_dve, False)
                    C.leave("turn", TURNS)
                for j in range(KD // 2):
                    pair(G22, KF, (4 + 2 * (j % 2), 5 + 2 * (j % 2)), act_hi, act_lo, for_dve, j == 0)

            pe.wait_ge(consts_made, 5)
            pe.wait_ge(x_loaded, 16)
            for t in range(KD):
                for n in range(KS):
                    ins = pe.transpose(ps[:, t, n * P:(n + 1) * P], x_tok[:, n, t * P:(t + 1) * P], ident[:, :])
                ins.then_inc(for_dve, C.made(for_dve))
                C.step(bank_read[t])

            with pe.Fori(0, DEPTH) as l:
                C.enter("layer", PER_LAYER, l)
                ffn()
                summed(0)
                for t in range(0, KR - 1, 2):
                    pair(G8, KD, (mix_bank(XR_T + t), mix_bank(XR_T + t + 1)), h_hi, h_lo, for_act, t == 0)
                single(mix_bank(XR_T + KR - 1), h_hi, h_lo, for_act)
                seen = 0
                for n, (m, g, kk) in enumerate(BANDS):
                    if n % BPC == 0:
                        s = chunk()
                    while seen <= kk:
                        pe.wait_ge(split_lo, C.next(split_lo))
                        seen += 1
                    b = mix_bank(RG_T + 2 * m + g)
                    first = n == 0 or BANDS[n - 1][:2] != (m, g)
                    last = n + 1 == len(BANDS) or BANDS[n + 1][:2] != (m, g)
                    if first:
                        pe.wait_ge(bank_read[b], C.now(bank_read[b]))
                    ins = product(b, *columns(s, n % BPC * P, 0), u_hi[:, kk, :], u_lo[:, kk, :], first, last)
                    if last:
                        ins.then_inc(for_act, C.made(for_act))
                        C.step(bank_read[b])
                for t in range(0, KR - 1, 2):
                    pair(G8, KD, (mix_bank(YR_T + t), mix_bank(YR_T + t + 1)), h_hi, h_lo, for_dve, False)
                single(mix_bank(YR_T + KR - 1), h_hi, h_lo, for_dve)
                for t in range(0, 2 * KD, 2):
                    pair(G8, KD, (mix_bank(G_T + t), mix_bank(G_T + t + 1)), h_hi, h_lo, for_act, False)
                for t in range(0, KD, 2):
                    pair(UP_A[t // 2], KR, (mix_bank(UA_T + t), mix_bank(UA_T + t + 1)), ya_hi, ya_lo, for_dve,
                         t == 0)

                def head_sums(t):
                    for n in (t, t + 1):
                        pe.wait_ge(square_made, C.next(square_made))
                        pe.wait_ge(bank_read[n % 2], C.now(bank_read[n % 2]))
                        pe.matmul(ps[:, n % 2, :], ones_head[:, :], square[:, n % 2, :], start=True, stop=True
                                  ).then_inc(square_used, 1)
                        C.step(bank_read[n % 2])

                for t in range(0, 2 * KD, 2):
                    pair(G8, KD, (mix_bank(QK_T + t), mix_bank(QK_T + t + 1)), h_hi, h_lo, for_act, False)
                    if t:
                        head_sums(t - 2)
                head_sums(2 * KD - 2)

                for half in range(2):
                    for a in range(0, KD, 2):
                        s = chunk()
                        for t in range(KS):
                            b = mix_bank(V_T + half * KS + t)
                            if a == 0:
                                pe.wait_ge(bank_read[b], C.now(bank_read[b]))
                            for kk in (a, a + 1):
                                at = (kk - a) * S
                                tok = slice(t * P, (t + 1) * P)
                                w = whi[:, s, at:at + S]
                                ins = pe.matmul(ps[:, b, :], h_lo[:, kk, tok], w, start=kk == 0, stop=False)
                                if not begun[0]:
                                    ins.then_inc(chunk_begun, C.made(chunk_begun))
                                    begun[0] = True
                                pe.matmul(ps[:, b, :], h_hi[:, kk, tok], w, start=False, stop=False)
                                ins = pe.matmul(ps[:, b, :], h_hi[:, kk, tok], wlo[:, s, at:at + S], start=False,
                                                stop=kk == KD - 1)
                            if a == KD - 2:
                                ins.then_inc(for_dve, C.made(for_dve))
                                C.step(bank_read[b])

                for b in range(8):
                    pe.wait_ge(bank_read[b], C.now(bank_read[b]))
                pe.wait_ge(qk_made, C.next(qk_made, 2 * KD))

                def scores(head):
                    t = head // 2
                    if head != 1:
                        pe.wait_ge(q_placed, C.next(q_placed, 1 if head else 4))
                    for i in range(KS):
                        pe.wait_ge(bank_read[i], C.now(bank_read[i]))
                        pe.matmul(ps[:, i, 0:(i + 1) * P], square[:, head % 2, i * P:(i + 1) * P],
                                  k[:, t, 0:(i + 1) * P], start=True, stop=True
                                  ).then_inc(for_dve, C.made(for_dve))
                        C.step(bank_read[i])

                scores(0)
                scores(1)
                for head in range(HEADS):
                    p_ = (head % 2) * HD
                    pe.wait_ge(prob_made, C.next(prob_made, KS))
                    for b, _, _, keys in TURNED:
                        pe.wait_ge(bank_read[b], C.now(bank_read[b]))
                        at = 0
                        for j in keys:
                            for i in range(j, KS):
                                ins = pe.transpose(ps[:, b, at:at + P],
                                                   prob[head % 2][:, tri(i) + j * P:tri(i) + (j + 1) * P], ident[:, :])
                                at += P
                        ins.then_inc(for_act, C.made(for_act))
                        C.step(bank_read[b])
                    if head + 2 < HEADS:
                        scores(head + 2)
                    if head % 2 == 0:
                        pe.wait_ge(bank_read[6], C.now(bank_read[6]))
                    for b, at, _, keys in TURNED:
                        pe.wait_ge(bank_read[b], C.now(bank_read[b]))
                        for j in keys:
                            ins = pe.matmul(ps[p_:p_ + HD, 6, j * P:S], v[j][:, head * HD:(head + 1) * HD],
                                            pt[:, at:at + (KS - j) * P], start=j == 0, stop=j == TURNED[-1][3][-1])
                            at += (KS - j) * P
                    if head % 2:
                        ins.then_inc(for_act, C.made(for_act))
                        C.step(bank_read[6])

                pe.wait_ge(bank_read[6], C.now(bank_read[6]))
                for t in range(0, KD, 2):
                    pair(G8, KD, (mix_bank(UB_T + t), mix_bank(UB_T + t + 1)), h_hi, h_lo, for_dve, False)
                for t in range(0, KD, 2):
                    pair(G8, KD, (mix_bank(OUT_T + t), mix_bank(OUT_T + t + 1)), m_hi, m_lo, for_dve, t == 0)
                ffn()
                C.leave("layer", DEPTH)

            for b in range(1, 8):
                pe.wait_ge(bank_read[b], C.now(bank_read[b]))
            for t in range(KS):
                for half in range(2):
                    for n in range(KD // 2):
                        ins = pe.transpose(ps[:, 2 * t + half, n * P:(n + 1) * P],
                                           x[:, half * (KD // 2) + n, t * P:(t + 1) * P], ident[:, :])
                    ins.then_inc(for_dve if half else for_act, C.made(for_dve if half else for_act))


def tri(i):
    return P * (i * (i + 1) // 2)


def kernel(**inputs):
    import concourse.bacc as bacc
    from concourse.bass_utils import run_bass_kernel_spmd as run

    a = {n: np.ascontiguousarray(v) for n, v in inputs.items()}

    def tiles(v):
        return v.reshape(DEPTH, -1, P).transpose(0, 2, 1)

    conv = a["conv_w"].reshape(DEPTH, CONV * RNN)
    params = np.concatenate(
        [tiles(a_) for a_ in (np.roll(a["norm_ffn1"], -1, axis=0), a["norm_mix"], a["norm_ffn2"], a["gate_bias"])] + [tiles(conv)]
        + [tiles(a[n]) for n in ("conv_b", "rg_b_a", "rg_b_x", "rg_lambda")]
        + [np.concatenate([a[n], a[n]], axis=1)[:, :, None] for n in ("q_gain", "k_gain")], axis=2)
    band = np.zeros((DEPTH, P, len(BANDS) * P), np.float32)
    for n, (m, g, kk) in enumerate(BANDS):
        for blk in range(RNN // RB):
            r0, r1 = max(blk * RB, kk * P), min((blk + 1) * RB, (kk + 1) * P)
            c0, c1 = max(blk * RB, m * P), min((blk + 1) * RB, (m + 1) * P)
            if r0 < r1 and c0 < c1:
                w = a["rg_w_x" if g else "rg_w_a"]
                band[:, r0 - kk * P:r1 - kk * P, n * P + c0 - m * P:n * P + c1 - m * P] = \
                    w[:, blk, r0 - blk * RB:r1 - blk * RB, c0 - blk * RB:c1 - blk * RB]
    rel = a["rel_table"][:, :, ::-1].reshape(DEPTH * HEADS, RELW)
    arrays = {
        "x": a["x"], "w_gate1": a["ffn1_w_gate"], "w_up1": a["ffn1_w_up"], "w_down1": a["ffn1_w_down"],
        "w_in": a["w_in"], "rg_band": band, "w_up_a": a["w_up_a"], "w_up_b": a["w_up_b"], "w_out": a["w_out"],
        "w_gate2": a["ffn2_w_gate"], "w_up2": a["ffn2_w_up"], "w_down2": a["ffn2_w_down"], "params": params,
        "rel_rev": rel, "first_gain": tiles(a["norm_ffn1"])[0],
    }
    arrays = {f"in_{n}": np.ascontiguousarray(v) for n, v in arrays.items()}
    nc = bacc.Bacc("TRN2", target_bir_lowering=False, num_devices=1)
    args = [nc.dram_tensor(n, v.shape, mybir.dt.from_np(v.dtype), kind="ExternalInput").ap()
            for n, v in arrays.items()]
    args.append(nc.dram_tensor("out", (1, S, D), F32, kind="ExternalOutput").ap())
    trunk(nc, *args)
    return run(nc, [arrays], core_ids=[0]).results[0]["out"]
```

```python
from contextlib import ExitStack

import numpy as np
import concourse.bass as bass
from concourse import mybir

F32, F32R = mybir.dt.float32, mybir.dt.float32r
ACT, ALU = mybir.ActivationFunctionType, mybir.AluOpType

P = 128
D, S, DEPTH = 1024, 512, 2
HEADS, HD, CHUNK = 16, 64, 64
REL_CLIP, CONV, LRU_C, EPS = 128, 4, 8.0, 1e-6
RNN = ((4 * D // 3 + P - 1) // P) * P
RB = RNN // 16
FF = ((8 * D // 3 + P - 1) // P) * P
KD, KR, KF, KS = D // P, RNN // P, FF // P, S // P
PAIR = 2 * P
TURNS = FF // PAIR
SLOTS, AHEAD = 4, 3
CW = 4 * PAIR

XR0, YR0, Q0 = 0, RNN, 2 * RNN
K0, V0, G0 = Q0 + D, Q0 + 2 * D, Q0 + 3 * D

BANDS = [(m, g, k) for m in range(KR) for g in range(2) for k in (m - 1, m, m + 1) if 0 <= k < KR]
BPC = CW // P
RG_CHUNKS = -(-len(BANDS) // BPC)

G8 = [(0, 4), (4, 8)]
G22 = [(0, 4), (4, 8), (8, 12), (12, 16), (16, 20), (20, 22)]
G11A = [(0, 4), (4, 8), (8, 11)]
G11B = [(0, 3), (3, 6), (6, 9), (9, 11)]
UP_A = [G11A, G11A, G11B, G11B]
XR_CHUNKS = (KR // 2) * len(G8) + 1
FFN_CHUNKS = TURNS * 4 + (KD // 2) * len(G22)
MIX_CHUNKS = 2 * XR_CHUNKS + RG_CHUNKS + sum(map(len, UP_A)) + 2 * KD + 2 * KD + KD + KD + KD
CHUNKS = 2 * FFN_CHUNKS + MIX_CHUNKS
BEFORE_ATTENTION = FFN_CHUNKS + MIX_CHUNKS - 2 * KD

PAR, NPAR = {}, 0
for _name, _n in (("ffn1_next", KD), ("mix", KD), ("ffn2", KD), ("gate", 2 * KD), ("conv_w", CONV * KR),
                  ("conv_b", KR), ("b_a", KR), ("b_x", KR), ("lam", KR), ("q_gain", 1), ("k_gain", 1)):
    PAR[_name] = NPAR
    NPAR += _n

RELW = 2 * REL_CLIP + 1
RELPAD = 3 * P - 1
RELROW = 5 * P

TURNED = [(4, 0, KS * P, (0,)), (5, KS * P, KS * P, (1, 3)), (7, 2 * KS * P, 2 * P, (2,))]

HALF_LN2 = 0.5 * float(np.log(2.0))
TINY = 1e-37

PER_TURN = {"hi_made": 4, "lo_made": 4, "chunk_begun": 4, "for_dve": 4, "silu_made": 2, "to_split": 2,
            "split_hi": 2, "split_lo": 2,
            **{f"bank_read{b}": 1 for b in range(4)}, **{f"raw_loaded{s}": 16 for s in range(SLOTS)}}
PER_LAYER = {
    "hi_made": CHUNKS, "lo_made": CHUNKS, "chunk_begun": CHUNKS, "for_act": 121, "for_dve": 211,
    "silu_made": 4 * TURNS,
    "square_made": 3 * KD + 2 * KD, "square_used": 3 * KD + 2 * KD, "rstd_made": 3,
    "to_split": 3 * KD + 4 * TURNS + KR + KD, "split_hi": 106, "split_lo": 98,
    "conv_begun": KR, "gated": KR, "tanh_made": KR, "logs_made": KR, "diff_made": KR, "drive_made": KR,
    "conv_step": 2 * KR, "scan_step": 2 * KR, "soft_step": 18, "lam_exp": 1, "decay_made": 1,
    "gelu_made": KR, "qk_made": 2 * KD, "qk_rstd": 2 * KD, "band_masked": 1, "q_placed": HEADS + 2,
    "exp_made": HEADS * KS, "prob_made": HEADS * KS, "inv_made": HEADS,
    "bank_read0": 47, "bank_read1": 46, "bank_read2": 56, "bank_read3": 56,
    "bank_read4": 41, "bank_read5": 39, "bank_read6": 29, "bank_read7": 37,
    **{f"raw_loaded{s}": 16 * CHUNKS // SLOTS for s in range(SLOTS)},
    "band_loaded0": 16 * HEADS, "band_loaded1": 16 * HEADS, "par_loaded": 16}


class Count:

    def __init__(self, start):
        self.n, self.loops = start, {}

    def value(self):
        v = self.n
        for reg, per in self.loops.values():
            v = reg * per + v
        return v


class Counts:

    def __init__(self, sems, starts):
        self.names = {id(s): n for n, s in sems.items()}
        self.all = {n: Count(starts.get(n, 0)) for n in sems}
        self.open = {}

    def step(self, sem, by=1):
        self.all[self.names[id(sem)]].n += by

    def made(self, sem, by=1):
        self.step(sem, by)
        return by

    def now(self, sem, back=0):
        self.step(sem, -back)
        v = self.all[self.names[id(sem)]].value()
        self.step(sem, back)
        return v

    def next(self, sem, by=1):
        self.step(sem, by)
        return self.now(sem)

    def enter(self, kind, table, reg, first=0):
        self.open[kind] = (table, first, {n: c.n for n, c in self.all.items()})
        for n, c in self.all.items():
            c.loops[kind] = (reg, table.get(n, 0))
            c.n -= first * table.get(n, 0)

    def leave(self, kind, passes):
        table, first, before = self.open.pop(kind)
        for n, c in self.all.items():
            per = table.get(n, 0)
            made = c.n + first * per - before[n]
            assert made in (0, per), (kind, n, made, per)
            c.n = before[n] + made * (passes - first)
            del c.loops[kind]


def trunk(nc, x_in, w_gate1, w_up1, w_down1, w_in, rg_band, w_up_a, w_up_b, w_out, w_gate2, w_up2, w_down2,
          params, rel_rev, first_gain, out):
    rel_rows = nc.dram_tensor("rel_rows", (DEPTH * HEADS, RELROW), F32)
    rel_band = nc.dram_tensor("rel_band", (DEPTH * HEADS, P, S), F32)

    ctx = ExitStack()
    with ctx:
        def sb(name, shape, dt=F32):
            return ctx.enter_context(nc.sbuf_tensor(name, shape, dt))

        def sem(name):
            return ctx.enter_context(nc.semaphore(name))

        x = sb("x", [P, KD, S])
        h_hi, h_lo = sb("h_hi", [P, KD, S], F32R), sb("h_lo", [P, KD, S], F32R)
        raw = sb("raw", [P, SLOTS, CW])
        whi, wlo = sb("whi", [P, SLOTS, CW], F32R), sb("wlo", [P, SLOTS, CW], F32R)
        tmp = sb("tmp", [P, 2, S])
        square = sb("square", [P, 2, S])
        rstd = square[:, 0, :]
        next_gain = sb("next_gain", [P, KD])
        ident, ones, ones_head = sb("ident", [P, P]), sb("ones", [P, P]), sb("ones_head", [P, P])
        par = sb("par", [P, NPAR])
        decay = sb("decay", [P, 2, KR])
        soft = sb("soft", [P, 4, KR])
        qg = sb("qg", [P, 1])
        carrier = sb("carrier", [1, HEADS * KS])
        mx, total, inv = sb("mx", [P, 2, KS]), sb("total", [P, 2, KS]), sb("inv", [P, 2, KS])

        def views(*parts):
            made = []
            with ExitStack() as scope:
                for n, (name, shape, dt) in enumerate(parts):
                    made.append(scope.enter_context(nc.sbuf_tensor(name, shape, dt)))
            return made

        R = KR * S
        act_hi, act_lo, gate, _ = views(("act_hi", [P, KF, S], F32R), ("act_lo", [P, KF, S], F32R),
                                        ("gate", [P, 2, S], F32), ("pad_f", [P, 2048], F32))
        u, u_hi, u_lo, r = views(("u", [P, KR, S], F32), ("u_hi", [P, KR, S], F32R), ("u_lo", [P, KR, S], F32R),
                                 ("r", [P, KR, S], F32))
        _, scan, y = views(("pad_a", [P, R], F32), ("scan", [P, KR, S], F32), ("y", [P, KR, S], F32))
        ya_hi, _, ya_lo = views(("ya_hi", [P, KR, S], F32R), ("pad_b", [P, 2 * R], F32), ("ya_lo", [P, KR, S], F32R))
        TRI = P * (KS * (KS + 1) // 2)
        q, v3, _, ya_out, pt, _, gb_out, p0, _, k, p1, _, v012 = views(
            ("q", [P, KD, S], F32), ("v3", [P, D], F32), ("pad_c", [P, R - KD * S - D], F32),
            ("ya_out", [P, KD, S], F32), ("pt", [P, TRI], F32), ("pad_d", [P, R - KD * S - TRI], F32),
            ("gb_out", [P, KD, S], F32), ("p0", [P, TRI], F32), ("pad_e", [P, R - KD * S - TRI], F32),
            ("k", [P, KD, S], F32), ("p1", [P, TRI], F32), ("pad_g", [P, R - KD * S - TRI], F32),
            ("v012", [P, 3, D], F32))
        m_hi, _, m_lo = views(("m_hi", [P, KD, S], F32R), ("pad_h", [P, 3 * R - KD * S], F32),
                              ("m_lo", [P, KD, S], F32R))
        x_tok, rel_t = views(("x_tok", [P, KS, D], F32), ("rel_t", [DEPTH * HEADS, RELROW], F32))
        y_tok, = views(("y_tok", [P, KS, D], F32))
        prob = [p0, p1]
        qk = [q, k]
        v = [v012[:, 0, :], v012[:, 1, :], v012[:, 2, :], v3[:, :]]

        ps = ctx.enter_context(nc.psum_tensor("ps", [P, 8, S], F32))

        hi_made, lo_made, chunk_begun = sem("hi_made"), sem("lo_made"), sem("chunk_begun")
        raw_loaded = [sem(f"raw_loaded{s}") for s in range(SLOTS)]
        for_act, for_dve = sem("for_act"), sem("for_dve")
        bank_read = [sem(f"bank_read{b}") for b in range(8)]
        silu_made = sem("silu_made")
        square_made, square_used, rstd_made = sem("square_made"), sem("square_used"), sem("rstd_made")
        to_split, split_hi, split_lo = sem("to_split"), sem("split_hi"), sem("split_lo")
        conv_begun, conv_step, gated, tanh_made = sem("conv_begun"), sem("conv_step"), sem("gated"), sem("tanh_made")
        logs_made, diff_made, drive_made = sem("logs_made"), sem("diff_made"), sem("drive_made")
        scan_step, soft_step = sem("scan_step"), sem("soft_step")
        lam_exp, decay_made = sem("lam_exp"), sem("decay_made")
        gelu_made, qk_made, qk_rstd = sem("gelu_made"), sem("qk_made"), sem("qk_rstd")
        exp_made, prob_made, inv_made = sem("exp_made"), sem("prob_made"), sem("inv_made")
        band_masked = sem("band_masked")
        q_placed = sem("q_placed")
        band_loaded = [sem(f"band_loaded{n}") for n in range(2)]
        par_loaded = sem("par_loaded")
        counted = {
            "hi_made": hi_made, "lo_made": lo_made, "chunk_begun": chunk_begun, "for_act": for_act,
            "silu_made": silu_made, "for_dve": for_dve, "square_made": square_made, "square_used": square_used,
            "rstd_made": rstd_made,
            "to_split": to_split, "split_hi": split_hi, "split_lo": split_lo, "conv_begun": conv_begun,
            "conv_step": conv_step, "gated": gated, "tanh_made": tanh_made, "logs_made": logs_made,
            "diff_made": diff_made, "drive_made": drive_made, "scan_step": scan_step, "soft_step": soft_step,
            "lam_exp": lam_exp, "decay_made": decay_made, "gelu_made": gelu_made, "qk_made": qk_made,
            "qk_rstd": qk_rstd, "exp_made": exp_made, "prob_made": prob_made, "inv_made": inv_made,
            "band_masked": band_masked, "q_placed": q_placed, "par_loaded": par_loaded,
            **{f"bank_read{b}": bank_read[b] for b in range(8)},
            **{f"raw_loaded{s}": raw_loaded[s] for s in range(SLOTS)},
            **{f"band_loaded{n}": band_loaded[n] for n in range(2)}}
        par_free, gain_loaded = sem("par_free"), sem("gain_loaded")
        x_loaded = [sem(f"x_loaded{n}") for n in range(KS)]
        rel_loaded, rel_padded, rel_stored, consts_made = (
            sem("rel_loaded"), sem("rel_padded"), sem("rel_stored"), sem("consts_made"))
        out_made, out_stored = [sem(f"out_made{h}") for h in range(2)], sem("out_stored")

        STARTS = {"lo_made": SLOTS}

        def counts(**starts):
            return Counts(counted, {**STARTS, **starts})

        def mix_bank(n):
            return 2 + n % 6

        XR_T, RG_T, YR_T, G_T, UA_T, QK_T = np.cumsum([0, KR, 2 * KR, KR, 2 * KD, KD]).tolist()
        V_BANKS = [2, 3, 4, 5, 6, 7, 4, 5]
        UB_T, OUT_T = 0, KD

        block = ctx.enter_context(nc.Block())

        @block.sync
        def _(sp):
            C = counts(lo_made=0)
            place = [0]

            def load(src, shape):
                s = place[0] % SLOTS
                place[0] += 1
                sp.wait_ge(lo_made, C.next(lo_made))
                n = int(np.prod(shape))
                dst = raw[:, s, 0:n].rearrange("p (a b) -> p a b", a=shape[0]) if len(shape) == 2 else raw[:, s, 0:n]
                sp.dma_start(dst, src).then_inc(raw_loaded[s], 16)

            def rows(w, kt):
                return w.rearrange("l (k p) n -> p (l k) n", p=P)

            def pairs(w, kt, l, col, n_pairs, groups):
                v_ = rows(w, kt)
                for j in range(n_pairs):
                    for a, b in (groups[j] if isinstance(groups[0], list) else groups):
                        load(v_[:, bass.ds(l * kt + a, b - a), col + j * PAIR:col + (j + 1) * PAIR], (b - a, PAIR))

            def ffn(w_gate, w_up, w_down, l):
                g_, u_ = rows(w_gate, KD), rows(w_up, KD)
                with sp.Fori(0, TURNS) as i:
                    C.enter("turn", PER_TURN, i)
                    for w in (g_, u_):
                        for a, b in G8:
                            load(w[:, bass.ds(l * KD + a, 4), bass.ds(i * PAIR, PAIR)], (4, PAIR))
                    C.leave("turn", TURNS)
                pairs(w_down, KF, l, 0, KD // 2, G22)

            x_t = x_in.rearrange("b (t p) d -> p (b t) d", p=P)
            for n in range(KS):
                sp.dma_start(x_tok[:, n, :], x_t[:, n, :]).then_inc(x_loaded[n], 16)
            sp.dma_start(next_gain[:, :], first_gain).then_inc(gain_loaded, 16)
            sp.dma_start(rel_t[:, RELPAD:RELPAD + RELW], rel_rev).then_inc(rel_loaded, 16)

            with sp.Fori(0, DEPTH) as l:
                C.enter("layer", PER_LAYER, l)
                sp.wait_ge(par_free, l + 1)
                sp.dma_start(par[:, :].rearrange("p (a n) -> p a n", a=1),
                             params.rearrange("l p n -> p l n")[:, bass.ds(l, 1), :]).then_inc(par_loaded, 16)
                ffn(w_gate1, w_up1, w_down1, l)
                win = rows(w_in, KD)
                for base, band in ((XR0, False), (0, True), (YR0, False)):
                    if band:
                        bands = rg_band.rearrange("l p n -> p l n")
                        for c in range(RG_CHUNKS):
                            n = min(CW, len(BANDS) * P - c * CW)
                            load(bands[:, bass.ds(l, 1), c * CW:c * CW + n], (1, n))
                    else:
                        pairs(w_in, KD, l, base, KR // 2, G8)
                        load(win[:, bass.ds(l * KD, KD), base + (KR - 1) * P:base + KR * P], (KD, P))
                pairs(w_in, KD, l, G0, KD, G8)
                pairs(w_up_a, KR, l, 0, KD // 2, UP_A)
                pairs(w_in, KD, l, Q0, KD, G8)
                sp.wait_ge(band_masked, C.next(band_masked))
                sp.wait_ge(rel_stored, 32)

                def band_of(head):
                    if head >= 2:
                        sp.wait_ge(exp_made, C.next(exp_made, KS))
                    band = rel_band[:, :, :].rearrange("h p n -> p h n")[:, bass.ds(l * HEADS + head, 1), :]
                    for p_, w_ in ((0, S - CHUNK), (CHUNK, S)):
                        sp.dma_start(tmp[p_:p_ + CHUNK, head % 2, 0:w_].rearrange("p (a n) -> p a n", a=1),
                                     band[p_:p_ + CHUNK, :, 0:w_]).then_inc(band_loaded[head % 2], 16)

                band_of(0)
                band_of(1)
                for half in range(2):
                    for a in range(0, KD, 2):
                        load(win[:, bass.ds(l * KD + a, 2), V0 + half * S:V0 + (half + 1) * S], (2, S))
                pairs(w_up_b, KD, l, 0, 2, G8)
                for head in range(2, HEADS):
                    band_of(head)
                C.step(exp_made, 2 * KS)
                v_ = rows(w_up_b, KD)
                for j in range(2, KD // 2):
                    for a, b in G8:
                        load(v_[:, bass.ds(l * KD + a, b - a), j * PAIR:(j + 1) * PAIR], (b - a, PAIR))
                pairs(w_out, KD, l, 0, KD // 2, G8)
                ffn(w_gate2, w_up2, w_down2, l)
                C.leave("layer", DEPTH)
            for _ in range(AHEAD):
                load(rows(w_up_b, KD)[:, 0:4, 0:PAIR], (4, PAIR))
            out_t = out.rearrange("b (t p) d -> p (b t) d", p=P)
            for t in range(KS):
                for half in range(2):
                    sp.wait_ge(out_made[half], t + 1)
                    at = slice(half * S, (half + 1) * S)
                    sp.dma_start(out_t[:, t, at], y_tok[:, t, at]).then_inc(out_stored, 16)
            sp.wait_ge(out_stored, 2 * KS * 16)

        @block.gpsimd
        def _(pool):
            C = counts()
            nc.gpsimd.memset(soft[:, 0, :], 0.0).then_inc(chunk_begun, AHEAD)
            nc.gpsimd.memset(soft[:, 1, :], 0.0).then_inc(square_used, 2)
            nc.gpsimd.memset(soft[:, 2, :], 0.0).then_inc(par_free, 1)
            nc.gpsimd.memset(ident[:, :], 0.0).then_inc(consts_made, 1)
            nc.gpsimd.memset(ones[:, :], 1.0).then_inc(lo_made, SLOTS)
            nc.gpsimd.memset(ones_head[:, :], 0.0).then_inc(consts_made, 1)
            pool.wait_ge(consts_made, 2)
            nc.gpsimd.affine_select(out=ident[:, :], in_=ident[:, :], compare_op=ALU.not_equal, fill=1.0, base=0,
                                    pattern=[[-1, P]], channel_multiplier=1).then_inc(consts_made, 1)
            nc.gpsimd.memset(ones_head[0:HD, 0:HD], 1.0).then_inc(consts_made, 1)
            pool.wait_ge(consts_made, 4)
            nc.gpsimd.memset(ones_head[HD:P, HD:P], 1.0).then_inc(consts_made, 1)
            pool.wait_ge(consts_made, 5)

            def lo(c, s):
                pool.wait_ge(hi_made, c + 1)
                nc.gpsimd.tensor_tensor(wlo[:, s, :], raw[:, s, :], whi[:, s, :].bitcast(F32), ALU.subtract
                                        ).then_inc(lo_made, 1)

            for c in range(AHEAD):
                lo(c, c)
            with pool.Fori(0, DEPTH) as l:
                C.enter("layer", PER_LAYER, l)
                with pool.Fori(0, BEFORE_ATTENTION // SLOTS - 1) as n:
                    for s in range(SLOTS):
                        lo(l * CHUNKS + n * SLOTS + (AHEAD + s), (AHEAD + s) % SLOTS)
                pool.wait_ge(qk_made, C.next(qk_made, 2 * KD))
                for head in range(HEADS):
                    if head == 2:
                        pool.wait_ge(q_placed, C.now(q_placed))
                        for s in range(SLOTS):
                            lo(l * CHUNKS + (BEFORE_ATTENTION - SLOTS + AHEAD + s), (AHEAD + s) % SLOTS)
                    if head >= 2:
                        pool.wait_ge(prob_made, C.next(prob_made, KS))
                    if head:
                        pool.wait_ge(q_placed, C.now(q_placed))
                    p_ = head % 2 * HD
                    zeros = ones_head[p_:p_ + HD, HD - p_:HD - p_ + 1].to_broadcast([HD, S])
                    nc.gpsimd.tensor_tensor(square[p_:p_ + HD, head % 2, :], q[p_:p_ + HD, head // 2, :], zeros,
                                            ALU.add).then_inc(q_placed, C.made(q_placed))
                    if head < 2:
                        nc.gpsimd.tensor_tensor(square[p_:p_ + HD, 1 - head % 2, :], zeros, zeros, ALU.add
                                                ).then_inc(q_placed, C.made(q_placed))
                C.step(prob_made, 2 * KS)
                with pool.Fori(0, (CHUNKS - BEFORE_ATTENTION) // SLOTS) as n:
                    for s in range(SLOTS):
                        lo(l * CHUNKS + n * SLOTS + (BEFORE_ATTENTION + AHEAD + s), (AHEAD + s) % SLOTS)
                C.leave("layer", DEPTH)

        @block.scalar
        def _(act):
            C = counts()
            place = [0]

            def ring(n=1):
                for _ in range(n):
                    s = place[0] % SLOTS
                    place[0] += 1
                    act.wait_ge(chunk_begun, C.next(chunk_begun))
                    act.wait_ge(raw_loaded[s], C.next(raw_loaded[s], 16))
                    nc.scalar.activation(whi[:, s, :], raw[:, s, :], ACT.Copy).then_inc(hi_made, C.made(hi_made))

            def col(name, j=0):
                return par[:, PAR[name] + j:PAR[name] + j + 1]

            def read(b, dst, func, **how):
                act.wait_ge(for_act, C.next(for_act))
                nc.scalar.activation(dst, ps[:, b, :], func, **how).then_inc(bank_read[b], C.made(bank_read[b]))

            def hi_of(dst, src):
                act.wait_ge(to_split, C.next(to_split))
                nc.scalar.activation(dst, src, ACT.Copy).then_inc(split_hi, C.made(split_hi))

            def squared(t, src):
                act.wait_ge(square_used, C.next(square_used))
                nc.scalar.activation(square[:, t % 2, :], src, ACT.Square).then_inc(square_made, C.made(square_made))

            def summed(ahead):
                C.step(square_used, ahead)
                act.wait_ge(square_used, C.now(square_used))
                C.step(square_used, -ahead)

            def rstd_from(b):
                act.preload_act_table_set("natural_log_exp_and_others")
                summed(2)
                nc.scalar.activation(rstd, ps[:, b, :], ACT.Ln, scale=1.0 / D, bias=EPS
                                     ).then_inc(bank_read[b], C.made(bank_read[b]))
                act.wait_ge(bank_read[b], C.now(bank_read[b]))
                nc.scalar.activation(rstd, rstd, ACT.Exp, scale=-0.5).then_inc(rstd_made, C.made(rstd_made))

            def renewed(t, b, to_ffn):
                C.step(bank_read[b])
                if to_ffn:
                    hi_of(h_hi[:, t, :], tmp[:, t % 2, :])
                else:
                    act.wait_ge(bank_read[b], C.now(bank_read[b]))
                if to_ffn or t < KD - 2:
                    squared(t, x[:, t, :])
                else:
                    C.step(square_used)
                    nc.scalar.activation(tmp[:, t % 2, :], x[:, t, :], ACT.Square
                                         ).then_inc(square_made, C.made(square_made))

            def ffn(to_ffn):
                with act.Fori(0, TURNS) as i:
                    C.enter("turn", PER_TURN, i)
                    ring(2)
                    for m in range(2):
                        C.step(bank_read[m])
                        act.wait_ge(bank_read[m], C.now(bank_read[m]))
                        nc.scalar.activation(gate[:, m, :], gate[:, m, :], ACT.Silu
                                             ).then_inc(silu_made, C.made(silu_made))
                    ring(2)
                    for m in range(2):
                        C.step(bank_read[2 + m])
                        hi_of(act_hi[:, :, :].rearrange("p k s -> p (k s)")[:, bass.ds((i * 2 + m) * S, S)],
                              tmp[:, m, :])
                    C.leave("turn", TURNS)
                for j in range(KD // 2):
                    ring(len(G22))
                    for t in (2 * j, 2 * j + 1):
                        renewed(t, 4 + t % 4, to_ffn)

            for t in range(KD + 1):
                if t < KD:
                    act.wait_ge(for_act, C.next(for_act))
                    nc.scalar.activation(x[:, t, :], ps[:, t, :], ACT.Copy
                                         ).then_inc(bank_read[t], C.made(bank_read[t]))
                if t:
                    C.step(bank_read[t - 1], -1)
                    renewed(t - 1, t - 1, True)
                if t % 2 and t < 2 * AHEAD:
                    ring()
                if t == 1:
                    act.wait_ge(rel_padded, 1)
                    act.dma_start(rel_rows[:, :], rel_t[:, :]).then_inc(rel_stored, 16)
            act.wait_ge(rel_stored, 16)
            act.dma_start(rel_band[:, :, :], bass.AP(rel_rows, P - 1, [[RELROW, DEPTH * HEADS], [-1, P], [1, S]])
                          ).then_inc(rel_stored, 16)

            with act.Fori(0, DEPTH) as l:
                C.enter("layer", PER_LAYER, l)
                C.step(par_loaded, 16)
                rstd_from(4)
                C.step(soft_step, 2)
                act.wait_ge(soft_step, C.now(soft_step))
                nc.scalar.activation(soft[:, 1, :], soft[:, 1, :], ACT.Exp, scale=-1.0
                                     ).then_inc(lam_exp, C.made(lam_exp))
                C.step(soft_step, 16)
                ffn(False)
                rstd_from(0)
                for t in range(KD):
                    hi_of(h_hi[:, t, :], tmp[:, t % 2, :])

                def conv_init(t):
                    act.wait_ge(for_act, C.next(for_act))
                    nc.scalar.activation(u[:, t, :], ps[:, mix_bank(XR_T + t), :], ACT.Identity,
                                         scale=col("conv_w", (CONV - 1) * KR + t), bias=col("conv_b", t)
                                         ).then_inc(conv_begun, C.made(conv_begun))
                    C.step(bank_read[mix_bank(XR_T + t)])

                def conv_hi(t):
                    act.wait_ge(bank_read[mix_bank(XR_T + t)], C.now(bank_read[mix_bank(XR_T + t)]))
                    nc.scalar.activation(u_hi[:, t, :], u[:, t, :], ACT.Copy).then_inc(split_hi, C.made(split_hi))

                for t in range(0, KR, 2):
                    ring()
                    if t:
                        conv_hi(t - 2)
                        conv_hi(t - 1)
                    if t + 1 < KR:
                        ring()
                        conv_init(t)
                        conv_init(t + 1)
                conv_init(KR - 1)
                conv_hi(KR - 1)

                blocks = chunks = 0
                for m in range(KR):
                    for g in range(2):
                        blocks += sum(b[:2] == (m, g) for b in BANDS)
                        while chunks * BPC < blocks:
                            ring()
                            chunks += 1
                        if g and m >= 2:
                            act.wait_ge(gated, C.next(gated))
                        read(mix_bank(RG_T + 2 * m + g), gate[:, m % 2, :] if g else r[:, m, :], ACT.Sigmoid,
                             bias=col("b_x" if g else "b_a", m))
                act.wait_ge(bank_read[mix_bank(RG_T + 2 * KR - 1)], C.now(bank_read[mix_bank(RG_T + 2 * KR - 1)]))
                act.wait_ge(decay_made, C.next(decay_made))

                for m in range(KR):
                    nc.scalar.activation(scan[:, m, :], r[:, m, :], ACT.Tanh, scale=decay[:, 0, m:m + 1]
                                         ).then_inc(tanh_made, C.made(tanh_made))
                    if m in (KR // 2, KR - 1):
                        ring()
                act.preload_act_table_set("natural_log_exp_and_others")
                act.wait_ge(tanh_made, C.now(tanh_made))
                for m in range(KR + 2):
                    if m >= 2:
                        act.wait_ge(diff_made, C.next(diff_made))
                        nc.scalar.activation(scan[:, m - 2, :], scan[:, m - 2, :], ACT.Exp, scale=0.5, bias=HALF_LN2
                                             ).then_inc(drive_made, C.made(drive_made))
                    if m < KR:
                        if m == 0:
                            act.wait_ge(gated, C.next(gated, 2))
                        nc.scalar.activation(gate[:, m % 2, :], scan[:, m, :], ACT.Ln, bias=1.0)
                        nc.scalar.activation(scan[:, m, :], scan[:, m, :], ACT.Ln, bias=TINY
                                             ).then_inc(logs_made, C.made(logs_made))
                        nc.scalar.activation(r[:, m, :], r[:, m, :], ACT.Exp, scale=decay[:, 1, m:m + 1])
                    if m % 2 and m <= KR:
                        ring()

                ring()
                for t in range(KR + 2):
                    if t < KR:
                        b = mix_bank(YR_T + t)
                        C.step(bank_read[b])
                        act.wait_ge(bank_read[b], C.now(bank_read[b]))
                        nc.scalar.activation(y[:, t, :], y[:, t, :], ACT.Gelu_apprx_tanh
                                             ).then_inc(gelu_made, C.made(gelu_made))
                    if t >= 2:
                        hi_of(ya_hi[:, t - 2, :], tmp[:, t % 2, :])
                    if t in (2, 5, 8, 10):
                        ring()
                for t in range(2 * KD):
                    if t % 2 == 0 and t:
                        ring(2)
                    read(mix_bank(G_T + t), ya_out[:, t, :] if t < KD else gb_out[:, t - KD, :], ACT.Sigmoid,
                         bias=col("gate", t))
                for j in range(KD // 2):
                    ring(len(UP_A[j]))
                for t in range(KD):
                    C.step(bank_read[mix_bank(UA_T + t)])

                act.preload_act_table_set("natural_log_exp_and_others")

                def head_rstd(t, ahead):
                    if t >= 2:
                        act.wait_ge(qk_made, C.next(qk_made))
                    summed(ahead)
                    nc.scalar.activation(gate[:, t % 2, :], ps[:, t % 2, :], ACT.Ln, scale=1.0 / HD, bias=EPS
                                         ).then_inc(bank_read[t % 2], C.made(bank_read[t % 2]))
                    act.wait_ge(bank_read[t % 2], C.now(bank_read[t % 2]))
                    nc.scalar.activation(gate[:, t % 2, :], gate[:, t % 2, :], ACT.Exp, scale=-0.5
                                         ).then_inc(qk_rstd, C.made(qk_rstd))

                for t in range(0, 2 * KD, 2):
                    ring(2)
                    for n in (t, t + 1):
                        b = mix_bank(QK_T + n)
                        act.wait_ge(for_act, C.next(for_act))
                        squared(n, ps[:, b, :])
                        nc.scalar.activation(qk[n // KD][:, n % KD, :], ps[:, b, :], ACT.Copy
                                             ).then_inc(bank_read[b], C.made(bank_read[b]))
                    if t:
                        head_rstd(t - 2, -1)
                        head_rstd(t - 1, 0)
                ring()
                head_rstd(2 * KD - 2, 1)
                head_rstd(2 * KD - 1, 2)
                C.step(qk_made, 2)

                for b in V_BANKS:
                    C.step(bank_read[b])

                def exps(head):
                    for i in range(KS):
                        C.step(bank_read[i])
                        act.wait_ge(bank_read[i], C.now(bank_read[i]))
                        part = prob[head % 2][:, tri(i):tri(i + 1)]
                        nc.scalar.activation(part, part, ACT.Exp, scale=-1.0, bias=mx[:, head % 2, i:i + 1],
                                             accum_out=total[:, head % 2, i:i + 1]
                                             ).then_inc(exp_made, C.made(exp_made))

                ring(6)
                exps(0)
                ring()
                exps(1)
                for head in range(HEADS):
                    for b, at, width, _ in TURNED:
                        act.wait_ge(for_act, C.next(for_act))
                        nc.scalar.activation(pt[:, at:at + width], ps[:, b, 0:width], ACT.Copy
                                             ).then_inc(bank_read[b], C.made(bank_read[b]))
                    if head + 2 < HEADS:
                        exps(head + 2)
                    if head % 2:
                        act.wait_ge(for_act, C.next(for_act))
                        nc.scalar.activation(h_hi[:, head // 2, :], ps[:, 6, :], ACT.Copy
                                             ).then_inc(split_hi, C.made(split_hi))
                        C.step(bank_read[6])

                for t in range(KD):
                    if t % 2 == 0:
                        ring(2)
                    C.step(bank_read[mix_bank(UB_T + t)])
                    hi_of(m_hi[:, t, :], tmp[:, t % 2, :])
                for t in range(KD):
                    if t % 2 == 0:
                        ring(2)
                    renewed(t, mix_bank(OUT_T + t), True)
                rstd_from(4)
                ffn(True)
                C.leave("layer", DEPTH)

            for t in range(KS):
                act.wait_ge(for_act, C.next(for_act))
                nc.scalar.activation(y_tok[:, t, 0:S], ps[:, 2 * t, :], ACT.Copy).then_inc(out_made[0], 1)

        @block.vector
        def _(dve):
            C = counts(square_used=2)

            def col(name, j=0):
                return par[:, PAR[name] + j:PAR[name] + j + 1]

            def lo_of(dst, src, hi):
                dve.wait_ge(split_hi, C.next(split_hi))
                nc.vector.tensor_tensor(dst, src, hi.bitcast(F32), ALU.subtract).then_inc(split_lo, C.made(split_lo))

            def added(t):
                dve.wait_ge(square_made, C.next(square_made, 2 if t == 1 else 1))
                if t > 1:
                    dve.wait_ge(square_used, C.now(square_used))
                nc.vector.tensor_tensor(square[:, t % 2, :], square[:, t % 2, :], square[:, (t + 1) % 2, :], ALU.add
                                        ).then_inc(square_used, C.made(square_used))

            def squares_behind(t):
                if 2 <= t < KD - 1:
                    added(t - 1)
                if t == KD - 1:
                    C.step(square_made, 2)
                    C.step(square_used, 3)

            def renewed(t, gain, first=False):
                if t >= 2 or not first:
                    dve.wait_ge(split_lo, C.now(split_lo))
                nc.vector.tensor_scalar(tmp[:, t % 2, :], x[:, t, :], gain, None, ALU.mult
                                        ).then_inc(to_split, C.made(to_split))
                if t >= 1:
                    lo_of(h_lo[:, t - 1, :], tmp[:, (t - 1) % 2, :], h_hi[:, t - 1, :])
                if t >= 2:
                    added(t - 1)
                if t == KD - 1:
                    lo_of(h_lo[:, t, :], tmp[:, t % 2, :], h_hi[:, t, :])
                    C.step(square_made)
                    C.step(square_used, 2)

            def norm(name):
                C.step(bank_read[0])
                dve.wait_ge(rstd_made, C.next(rstd_made))

                def scaled(t):
                    nc.vector.scalar_tensor_tensor(tmp[:, t % 2, :], x[:, t, :], col(name, t), rstd, ALU.mult,
                                                   ALU.mult).then_inc(to_split, C.made(to_split))

                scaled(0)
                scaled(1)
                for t in range(KD):
                    lo_of(h_lo[:, t, :], tmp[:, t % 2, :], h_hi[:, t, :])
                    if t + 2 < KD:
                        dve.wait_ge(split_lo, C.now(split_lo))
                        scaled(t + 2)

            def ffn(to_ffn):
                with dve.Fori(0, TURNS) as i:
                    C.enter("turn", PER_TURN, i)
                    for m in range(2):
                        dve.wait_ge(for_dve, C.next(for_dve))
                        nc.vector.tensor_tensor(gate[:, m, :], ps[:, m, :], rstd, ALU.mult
                                                ).then_inc(bank_read[m], C.made(bank_read[m]))
                    for m in range(2):
                        dve.wait_ge(split_lo, C.now(split_lo, 1 - m))
                        dve.wait_ge(for_dve, C.next(for_dve))
                        nc.vector.tensor_tensor(tmp[:, m, :], ps[:, 2 + m, :], rstd, ALU.mult
                                                ).then_inc(bank_read[2 + m], C.made(bank_read[2 + m]))
                    for m in range(2):
                        dve.wait_ge(silu_made, C.next(silu_made))
                        dve.wait_ge(bank_read[2 + m], C.now(bank_read[2 + m]))
                        nc.vector.tensor_tensor(tmp[:, m, :], tmp[:, m, :], gate[:, m, :], ALU.mult
                                                ).then_inc(to_split, C.made(to_split))
                    for m in range(2):
                        at = bass.ds((i * 2 + m) * S, S)
                        lo_of(act_lo[:, :, :].rearrange("p k s -> p (k s)")[:, at], tmp[:, m, :],
                              act_hi[:, :, :].rearrange("p k s -> p (k s)")[:, at])
                    C.leave("turn", TURNS)
                for t in range(KD):
                    dve.wait_ge(for_dve, C.next(for_dve))
                    nc.vector.scalar_tensor_tensor(x[:, t, :], ps[:, 4 + t % 4, :], 0.5, x[:, t, :], ALU.mult, ALU.add
                                                   ).then_inc(bank_read[4 + t % 4], C.made(bank_read[4 + t % 4]))
                    if to_ffn:
                        dve.wait_ge(bank_read[4 + t % 4], C.now(bank_read[4 + t % 4]))
                        renewed(t, next_gain[:, t:t + 1])
                    else:
                        squares_behind(t)

            dve.wait_ge(rel_loaded, 16)
            nc.vector.tensor_copy(rel_t[:, 0:RELPAD],
                                  rel_t[:, RELPAD:RELPAD + 1].to_broadcast([DEPTH * HEADS, RELPAD])
                                  ).then_inc(rel_padded, 1)
            dve.wait_ge(gain_loaded, 16)
            for t in range(KD):
                C.step(bank_read[t])
                dve.wait_ge(bank_read[t], C.now(bank_read[t]))
                renewed(t, next_gain[:, t:t + 1], True)

            with dve.Fori(0, DEPTH) as l:
                C.enter("layer", PER_LAYER, l)
                dve.wait_ge(par_loaded, C.next(par_loaded, 16))
                lam = par[:, PAR["lam"]:PAR["lam"] + KR]
                neg, z, c, e = (soft[:, n, :] for n in range(4))
                nc.vector.tensor_scalar(neg, lam, -1.0, None, ALU.mult).then_inc(soft_step, C.made(soft_step))
                dve.wait_ge(soft_step, C.now(soft_step))
                nc.vector.tensor_tensor(z, neg, lam, ALU.max).then_inc(soft_step, C.made(soft_step))
                C.step(bank_read[4])
                dve.wait_ge(rstd_made, C.next(rstd_made))
                dve.wait_ge(lam_exp, C.next(lam_exp))
                nc.vector.tensor_scalar(c, z, 2.0, None, ALU.add).then_inc(soft_step, C.made(soft_step))
                dve.wait_ge(soft_step, C.now(soft_step))
                nc.vector.reciprocal(c, c).then_inc(soft_step, C.made(soft_step))
                dve.wait_ge(soft_step, C.now(soft_step))
                nc.vector.tensor_tensor(z, z, c, ALU.mult).then_inc(soft_step, C.made(soft_step))
                dve.wait_ge(soft_step, C.now(soft_step))
                nc.vector.tensor_tensor(c, z, z, ALU.mult).then_inc(soft_step, C.made(soft_step))
                dve.wait_ge(soft_step, C.now(soft_step))
                nc.vector.tensor_scalar(e, c, 1.0 / 17, None, ALU.mult).then_inc(soft_step, C.made(soft_step))
                dve.wait_ge(soft_step, C.now(soft_step))
                for n in range(15, 1, -2):
                    nc.vector.scalar_tensor_tensor(e, e, 1.0 / n, c, ALU.add, ALU.mult
                                                   ).then_inc(soft_step, C.made(soft_step))
                    dve.wait_ge(soft_step, C.now(soft_step))
                nc.vector.scalar_tensor_tensor(e, e, 1.0, z, ALU.add, ALU.mult).then_inc(soft_step, C.made(soft_step))
                dve.wait_ge(soft_step, C.now(soft_step))
                nc.vector.tensor_scalar(neg, neg, 0.0, LRU_C, ALU.max, ALU.mult).then_inc(soft_step, C.made(soft_step))
                dve.wait_ge(soft_step, C.now(soft_step))
                nc.vector.scalar_tensor_tensor(decay[:, 0, :], e, 2 * LRU_C, neg, ALU.mult, ALU.add
                                               ).then_inc(soft_step, C.made(soft_step))
                dve.wait_ge(soft_step, C.now(soft_step))
                nc.vector.tensor_scalar(decay[:, 1, :], decay[:, 0, :], -1.0, None, ALU.mult
                                        ).then_inc(soft_step, C.made(soft_step))
                dve.wait_ge(soft_step, C.now(soft_step))
                nc.vector.tensor_scalar(qg[:, :], col("q_gain"), HD ** -0.5, None, ALU.mult
                                        ).then_inc(decay_made, C.made(decay_made))
                ffn(False)
                norm("mix")

                def conv(t):
                    b = mix_bank(XR_T + t)
                    dve.wait_ge(conv_begun, C.next(conv_begun))
                    for back in range(1, CONV):
                        ins = nc.vector.scalar_tensor_tensor(
                            u[:, t, back:S], ps[:, b, 0:S - back], col("conv_w", (CONV - 1 - back) * KR + t),
                            u[:, t, back:S], ALU.mult, ALU.add)
                        if back < CONV - 1:
                            ins.then_inc(conv_step, C.made(conv_step))
                            dve.wait_ge(conv_step, C.now(conv_step))
                        else:
                            ins.then_inc(bank_read[b], C.made(bank_read[b]))

                for t in range(0, KR, 2):
                    both = range(t, min(t + 2, KR))
                    for n in both:
                        conv(n)
                    for n in both:
                        lo_of(u_lo[:, n, :], u[:, n, :], u_hi[:, n, :])
                for m in range(KR):
                    C.step(bank_read[mix_bank(RG_T + 2 * m)])
                    C.step(bank_read[mix_bank(RG_T + 2 * m + 1)])
                    dve.wait_ge(bank_read[mix_bank(RG_T + 2 * m + 1)], C.now(bank_read[mix_bank(RG_T + 2 * m + 1)]))
                    nc.vector.tensor_tensor(u[:, m, :], u[:, m, :], gate[:, m % 2, :], ALU.mult
                                            ).then_inc(gated, C.made(gated))
                def yr_out(t):
                    dve.wait_ge(for_dve, C.next(for_dve))
                    nc.vector.tensor_copy(y[:, t, :], ps[:, mix_bank(YR_T + t), :]
                                      ).then_inc(bank_read[mix_bank(YR_T + t)], C.made(bank_read[mix_bank(YR_T + t)]))

                for m in range(KR + 3):
                    if m in (3, 7, 11):
                        yr_out((m - 3) // 2)
                        yr_out((m - 3) // 2 + 1)
                    if m < KR:
                        dve.wait_ge(logs_made, C.next(logs_made))
                        nc.vector.tensor_tensor(scan[:, m, :], scan[:, m, :], gate[:, m % 2, :], ALU.subtract
                                                ).then_inc(diff_made, C.made(diff_made))
                    if m >= 3:
                        n = m - 3
                        dve.wait_ge(drive_made, C.next(drive_made))
                        nc.vector.tensor_tensor(scan[:, n, :], scan[:, n, :], u[:, n, :], ALU.mult
                                                ).then_inc(scan_step, C.made(scan_step))
                        dve.wait_ge(scan_step, C.now(scan_step))
                        nc.vector.tensor_tensor_scan(scan[:, n, :], r[:, n, :], scan[:, n, :], 0.0, ALU.mult, ALU.add
                                                     ).then_inc(scan_step, C.made(scan_step))
                dve.wait_ge(scan_step, C.now(scan_step))

                def gated_h(t):
                    dve.wait_ge(gelu_made, C.next(gelu_made))
                    nc.vector.tensor_tensor(tmp[:, t % 2, :], y[:, t, :], scan[:, t, :], ALU.mult
                                            ).then_inc(to_split, C.made(to_split))

                yr_out(6)
                yr_out(7)
                gated_h(0)
                gated_h(1)
                for t in range(KR):
                    if t == 3:
                        yr_out(8)
                        yr_out(9)
                    if t == 6:
                        yr_out(10)
                    lo_of(ya_lo[:, t, :], tmp[:, t % 2, :], ya_hi[:, t, :])
                    if t + 2 < KR:
                        dve.wait_ge(split_lo, C.now(split_lo))
                        gated_h(t + 2)
                dve.wait_ge(split_lo, C.now(split_lo))
                nc.vector.memset(tmp[0:CHUNK, 0, S - CHUNK:S], -1e30)
                nc.vector.memset(tmp[0:CHUNK, 1, S - CHUNK:S], -1e30).then_inc(band_masked, C.made(band_masked))
                for t in range(2 * KD):
                    C.step(bank_read[mix_bank(G_T + t)])
                    if t == KD - 1:
                        dve.wait_ge(bank_read[mix_bank(G_T + t)], C.now(bank_read[mix_bank(G_T + t)]))
                for t in range(KD):
                    b = mix_bank(UA_T + t)
                    dve.wait_ge(for_dve, C.next(for_dve))
                    nc.vector.tensor_tensor(ya_out[:, t, :], ps[:, b, :], ya_out[:, t, :], ALU.mult
                                            ).then_inc(bank_read[b], C.made(bank_read[b]))

                C.step(square_made, 2 * KD)
                C.step(square_used, 2 * KD)

                def qk_scaled(t):
                    C.step(bank_read[t % 2])
                    dve.wait_ge(qk_rstd, C.next(qk_rstd))
                    part = qk[t // KD][:, t % KD, :]
                    nc.vector.scalar_tensor_tensor(part, part, col("k_gain") if t >= KD else qg[:, :],
                                                   gate[:, t % 2, :], ALU.mult, ALU.mult
                                                   ).then_inc(qk_made, C.made(qk_made))

                for t in range(2 * KD):
                    C.step(bank_read[mix_bank(QK_T + t)])
                    if t % 2 and t > 1:
                        qk_scaled(t - 3)
                        qk_scaled(t - 2)
                qk_scaled(2 * KD - 2)
                qk_scaled(2 * KD - 1)
                def biased(head):
                    dve.wait_ge(band_loaded[head % 2], C.next(band_loaded[head % 2], 32))
                    for i in range(KS):
                        dve.wait_ge(for_dve, C.next(for_dve))
                        nc.vector.memset(carrier[0:1, head * KS + i:head * KS + i + 1], 0.0)
                        nc.vector.tensor_tensor_reduce(prob[head % 2][:, tri(i):tri(i + 1)], ps[:, i, 0:(i + 1) * P],
                                                       tmp[:, head % 2, S - (i + 1) * P:S], -1.0, 3e38, ALU.add,
                                                       ALU.min, mx[:, head % 2, i:i + 1]
                                                       ).then_inc(bank_read[i], C.made(bank_read[i]))

                def normalised(head):
                    e = head % 2
                    dve.wait_ge(exp_made, C.next(exp_made, KS))
                    nc.vector.reciprocal(inv[:, e, :], total[:, e, :]).then_inc(inv_made, C.made(inv_made))
                    dve.wait_ge(inv_made, C.now(inv_made))
                    for i in range(KS):
                        part = prob[e][:, tri(i):tri(i + 1)]
                        nc.vector.tensor_scalar(part, part, inv[:, e, i:i + 1], None, ALU.mult
                                                ).then_inc(prob_made, C.made(prob_made))

                def v_out(half):
                    for t in range(KS):
                        b = V_BANKS[half * KS + t]
                        dve.wait_ge(for_dve, C.next(for_dve))
                        nc.vector.tensor_copy(v[t][:, half * S:(half + 1) * S], ps[:, b, :]
                                              ).then_inc(bank_read[b], C.made(bank_read[b]))

                dve.wait_ge(qk_made, C.now(qk_made))
                v_out(0)
                biased(0)
                biased(1)
                normalised(0)
                v_out(1)
                for head in range(HEADS):
                    if head + 1 < HEADS:
                        normalised(head + 1)
                    if head + 2 < HEADS:
                        biased(head + 2)
                    for b, *_ in TURNED:
                        C.step(bank_read[b])
                    if head % 2:
                        t = head // 2
                        dve.wait_ge(split_hi, C.next(split_hi))
                        nc.vector.tensor_tensor(h_lo[:, t, :], ps[:, 6, :], h_hi[:, t, :].bitcast(F32), ALU.subtract
                                                ).then_inc(bank_read[6], C.made(bank_read[6]))

                def merged(t):
                    b = mix_bank(UB_T + t)
                    dve.wait_ge(for_dve, C.next(for_dve))
                    nc.vector.tensor_tensor(tmp[:, t % 2, :], ps[:, b, :], gb_out[:, t, :], ALU.mult
                                            ).then_inc(bank_read[b], C.made(bank_read[b]))
                    dve.wait_ge(bank_read[b], C.now(bank_read[b]))
                    nc.vector.tensor_tensor(tmp[:, t % 2, :], tmp[:, t % 2, :], ya_out[:, t, :], ALU.add
                                            ).then_inc(to_split, C.made(to_split))

                merged(0)
                merged(1)
                for t in range(KD):
                    lo_of(m_lo[:, t, :], tmp[:, t % 2, :], m_hi[:, t, :])
                    if t + 2 < KD:
                        dve.wait_ge(split_lo, C.now(split_lo))
                        merged(t + 2)
                for t in range(KD):
                    b = mix_bank(OUT_T + t)
                    dve.wait_ge(for_dve, C.next(for_dve))
                    nc.vector.tensor_tensor(x[:, t, :], ps[:, b, :], x[:, t, :], ALU.add
                                            ).then_inc(bank_read[b], C.made(bank_read[b]))
                    dve.wait_ge(bank_read[b], C.now(bank_read[b]))
                    renewed(t, col("ffn2", t))
                C.step(bank_read[4])
                dve.wait_ge(rstd_made, C.next(rstd_made))
                nc.vector.tensor_copy(next_gain[:, :], par[:, PAR["ffn1_next"]:PAR["ffn1_next"] + KD]
                                      ).then_inc(par_free, 1)
                ffn(True)
                C.leave("layer", DEPTH)

            for t in range(KS):
                dve.wait_ge(for_dve, C.next(for_dve))
                nc.vector.tensor_copy(y_tok[:, t, S:D], ps[:, 2 * t + 1, :]).then_inc(out_made[1], 1)

        @block.tensor
        def _(pe):
            C = counts(square_used=2)
            place = [0]
            begun = [True]

            def chunk():
                s = place[0] % SLOTS
                place[0] += 1
                pe.wait_ge(lo_made, C.next(lo_made))
                begun[0] = False
                return s

            def product(b, w_hi, w_lo, x_hi, x_lo, start, stop):
                ins = pe.matmul(ps[:, b, :], w_hi, x_lo, start=start, stop=False)
                if not begun[0]:
                    ins.then_inc(chunk_begun, C.made(chunk_begun))
                    begun[0] = True
                pe.matmul(ps[:, b, :], w_hi, x_hi, start=False, stop=False)
                return pe.matmul(ps[:, b, :], w_lo, x_hi, start=False, stop=stop)

            def columns(s, at, m):
                return whi[:, s, at + m * P:at + (m + 1) * P], wlo[:, s, at + m * P:at + (m + 1) * P]

            def pair(groups, kt, banks, hi, lo, ready, wait, behind=None):
                for g, (a, z) in enumerate(groups):
                    s = chunk()
                    for m, b in enumerate(banks):
                        if g == 0:
                            pe.wait_ge(bank_read[b], C.now(bank_read[b]))
                        for kk in range(a, z):
                            if wait and m == 0:
                                pe.wait_ge(split_lo, C.next(split_lo))
                            ins = product(b, *columns(s, (kk - a) * PAIR, m), hi[:, kk, :], lo[:, kk, :],
                                          kk == 0, kk == kt - 1)
                        if g == len(groups) - 1:
                            ins.then_inc(ready, C.made(ready))
                            C.step(bank_read[b])
                    if behind:
                        behind(g)

            def single(b, hi, lo, ready):
                s = chunk()
                pe.wait_ge(bank_read[b], C.now(bank_read[b]))
                for kk in range(KD):
                    ins = product(b, *columns(s, kk * P, 0), hi[:, kk, :], lo[:, kk, :], kk == 0, kk == KD - 1)
                ins.then_inc(ready, C.made(ready))
                C.step(bank_read[b])

            def summed(b, parts):
                last = len(parts) - 1
                C.step(square_made, KD - last)
                pe.wait_ge(square_used, C.next(square_used, KD - last - 1))
                pe.wait_ge(bank_read[b], C.now(bank_read[b]))
                for n, part in enumerate(parts):
                    if n:
                        pe.wait_ge(square_made, C.next(square_made))
                    pe.matmul(ps[:, b, :], ones[:, :], part, start=n == 0, stop=n == last
                              ).then_inc(square_used, C.made(square_used))
                C.step(bank_read[b])

            def ffn():
                pair(G8, KD, (0, 1), h_hi, h_lo, for_dve, True,
                     lambda g: g == 0 and summed(4, [square[:, 0, :], square[:, 1, :]]))
                pair(G8, KD, (2, 3), h_hi, h_lo, for_dve, False)
                with pe.Fori(1, TURNS) as i:
                    C.enter("turn", PER_TURN, i, 1)
                    pair(G8, KD, (0, 1), h_hi, h_lo, for_dve, False)
                    pair(G8, KD, (2, 3), h_hi, h_lo, for_dve, False)
                    C.leave("turn", TURNS)
                for j in range(KD // 2):
                    pair(G22, KF, (4 + 2 * (j % 2), 5 + 2 * (j % 2)), act_hi, act_lo, for_dve, j == 0)

            pe.wait_ge(consts_made, 5)
            for n in range(KS):
                pe.wait_ge(x_loaded[n], 16)
                for t in range(KD):
                    ins = pe.transpose(ps[:, t, n * P:(n + 1) * P], x_tok[:, n, t * P:(t + 1) * P], ident[:, :])
                    if n == KS - 1:
                        ins.then_inc(for_act, C.made(for_act))
                        C.step(bank_read[t])

            with pe.Fori(0, DEPTH) as l:
                C.enter("layer", PER_LAYER, l)
                ffn()
                summed(0, [square[:, 1, :], tmp[:, 0, :], tmp[:, 1, :]])
                for t in range(0, KR - 1, 2):
                    pair(G8, KD, (mix_bank(XR_T + t), mix_bank(XR_T + t + 1)), h_hi, h_lo, for_act, t == 0)
                single(mix_bank(XR_T + KR - 1), h_hi, h_lo, for_act)
                seen = 0
                for n, (m, g, kk) in enumerate(BANDS):
                    if n % BPC == 0:
                        s = chunk()
                    while seen <= kk:
                        pe.wait_ge(split_lo, C.next(split_lo))
                        seen += 1
                    b = mix_bank(RG_T + 2 * m + g)
                    first = n == 0 or BANDS[n - 1][:2] != (m, g)
                    last = n + 1 == len(BANDS) or BANDS[n + 1][:2] != (m, g)
                    if first:
                        pe.wait_ge(bank_read[b], C.now(bank_read[b]))
                    ins = product(b, *columns(s, n % BPC * P, 0), u_hi[:, kk, :], u_lo[:, kk, :], first, last)
                    if last:
                        ins.then_inc(for_act, C.made(for_act))
                        C.step(bank_read[b])
                for t in range(0, KR - 1, 2):
                    pair(G8, KD, (mix_bank(YR_T + t), mix_bank(YR_T + t + 1)), h_hi, h_lo, for_dve, False)
                single(mix_bank(YR_T + KR - 1), h_hi, h_lo, for_dve)
                for t in range(0, 2 * KD, 2):
                    pair(G8, KD, (mix_bank(G_T + t), mix_bank(G_T + t + 1)), h_hi, h_lo, for_act, False)
                for t in range(0, KD, 2):
                    pair(UP_A[t // 2], KR, (mix_bank(UA_T + t), mix_bank(UA_T + t + 1)), ya_hi, ya_lo, for_dve,
                         t == 0)

                def head_sums(t):
                    for n in (t, t + 1):
                        pe.wait_ge(square_made, C.next(square_made))
                        pe.wait_ge(bank_read[n % 2], C.now(bank_read[n % 2]))
                        pe.matmul(ps[:, n % 2, :], ones_head[:, :], square[:, n % 2, :], start=True, stop=True
                                  ).then_inc(square_used, C.made(square_used))
                        C.step(bank_read[n % 2])

                for t in range(0, 2 * KD, 2):
                    pair(G8, KD, (mix_bank(QK_T + t), mix_bank(QK_T + t + 1)), h_hi, h_lo, for_act, False)
                    if t:
                        head_sums(t - 2)
                def scores(head):
                    t = head // 2
                    if head != 1:
                        pe.wait_ge(q_placed, C.next(q_placed, 1 if head else 4))
                    for i in range(KS):
                        pe.wait_ge(bank_read[i], C.now(bank_read[i]))
                        pe.matmul(ps[:, i, 0:(i + 1) * P], square[:, head % 2, i * P:(i + 1) * P],
                                  k[:, t, 0:(i + 1) * P], start=True, stop=True).then_inc(for_dve, C.made(for_dve))
                        C.step(bank_read[i])

                for half in range(2):
                    for a in range(0, KD, 2):
                        s = chunk()
                        for t in range(KS):
                            b = V_BANKS[half * KS + t]
                            if a == 0:
                                pe.wait_ge(bank_read[b], C.now(bank_read[b]))
                            for kk in (a, a + 1):
                                at = (kk - a) * S
                                tok = slice(t * P, (t + 1) * P)
                                w = whi[:, s, at:at + S]
                                ins = pe.matmul(ps[:, b, :], h_lo[:, kk, tok], w, start=kk == 0, stop=False)
                                if not begun[0]:
                                    ins.then_inc(chunk_begun, C.made(chunk_begun))
                                    begun[0] = True
                                pe.matmul(ps[:, b, :], h_hi[:, kk, tok], w, start=False, stop=False)
                                ins = pe.matmul(ps[:, b, :], h_hi[:, kk, tok], wlo[:, s, at:at + S], start=False,
                                                stop=kk == KD - 1)
                            if a == KD - 2:
                                ins.then_inc(for_dve, C.made(for_dve))
                                C.step(bank_read[b])
                        if (half, a) == (0, 0):
                            head_sums(2 * KD - 2)
                        if (half, a) == (1, 2):
                            pe.wait_ge(qk_made, C.next(qk_made, 2 * KD))
                            scores(0)
                        if (half, a) == (1, 4):
                            scores(1)

                for b in range(4, 8):
                    pe.wait_ge(bank_read[b], C.now(bank_read[b]))
                def up_b_begun(m):
                    b = mix_bank(UB_T + m)
                    pe.wait_ge(bank_read[b], C.now(bank_read[b]))
                    for kk in range(*G8[0]):
                        product(b, *columns(ub_slot, kk * PAIR, m), h_hi[:, kk, :], h_lo[:, kk, :], kk == 0, False)

                for head in range(HEADS):
                    p_ = (head % 2) * HD
                    pe.wait_ge(prob_made, C.next(prob_made, KS))
                    for b, _, _, keys in TURNED:
                        pe.wait_ge(bank_read[b], C.now(bank_read[b]))
                        at = 0
                        for j in keys:
                            for i in range(j, KS):
                                ins = pe.transpose(ps[:, b, at:at + P],
                                                   prob[head % 2][:, tri(i) + j * P:tri(i) + (j + 1) * P], ident[:, :])
                                at += P
                        ins.then_inc(for_act, C.made(for_act))
                        C.step(bank_read[b])
                    if head + 2 < HEADS:
                        scores(head + 2)
                    elif head + 2 == HEADS:
                        ub_slot = chunk()
                        up_b_begun(0)
                    else:
                        up_b_begun(1)
                    if head % 2 == 0:
                        pe.wait_ge(bank_read[6], C.now(bank_read[6]))
                    for b, at, _, keys in TURNED:
                        pe.wait_ge(bank_read[b], C.now(bank_read[b]))
                        for j in keys:
                            ins = pe.matmul(ps[p_:p_ + HD, 6, j * P:S], v[j][:, head * HD:(head + 1) * HD],
                                            pt[:, at:at + (KS - j) * P], start=j == 0, stop=j == TURNED[-1][3][-1])
                            at += (KS - j) * P
                    if head % 2:
                        ins.then_inc(for_act, C.made(for_act))
                        C.step(bank_read[6])

                pe.wait_ge(bank_read[6], C.now(bank_read[6]))
                s = chunk()
                for m in range(2):
                    b = mix_bank(UB_T + m)
                    for kk in range(*G8[1]):
                        ins = product(b, *columns(s, (kk - G8[1][0]) * PAIR, m), h_hi[:, kk, :], h_lo[:, kk, :],
                                      False, kk == KD - 1)
                    ins.then_inc(for_dve, C.made(for_dve))
                    C.step(bank_read[b])
                for t in range(2, KD, 2):
                    pair(G8, KD, (mix_bank(UB_T + t), mix_bank(UB_T + t + 1)), h_hi, h_lo, for_dve, False)
                for t in range(0, KD, 2):
                    pair(G8, KD, (mix_bank(OUT_T + t), mix_bank(OUT_T + t + 1)), m_hi, m_lo, for_dve, t == 0)
                ffn()
                C.leave("layer", DEPTH)

            for b in range(1, 8):
                pe.wait_ge(bank_read[b], C.now(bank_read[b]))
            for t in range(KS):
                for half in range(2):
                    for n in range(KD // 2):
                        ins = pe.transpose(ps[:, 2 * t + half, n * P:(n + 1) * P],
                                           x[:, half * (KD // 2) + n, t * P:(t + 1) * P], ident[:, :])
                    ins.then_inc(for_dve if half else for_act, C.made(for_dve if half else for_act))


def tri(i):
    return P * (i * (i + 1) // 2)


def kernel(**inputs):
    import concourse.bacc as bacc
    from concourse.bass_utils import run_bass_kernel_spmd as run

    a = {n: np.ascontiguousarray(v) for n, v in inputs.items()}

    def tiles(v):
        return v.reshape(DEPTH, -1, P).transpose(0, 2, 1)

    conv = a["conv_w"].reshape(DEPTH, CONV * RNN)
    params = np.concatenate(
        [tiles(v) for v in (np.roll(a["norm_ffn1"], -1, axis=0), a["norm_mix"], a["norm_ffn2"], a["gate_bias"])]
        + [tiles(conv)]
        + [tiles(a[n]) for n in ("conv_b", "rg_b_a", "rg_b_x", "rg_lambda")]
        + [np.concatenate([a[n], a[n]], axis=1)[:, :, None] for n in ("q_gain", "k_gain")], axis=2)
    band = np.zeros((DEPTH, P, len(BANDS) * P), np.float32)
    for n, (m, g, kk) in enumerate(BANDS):
        for blk in range(RNN // RB):
            r0, r1 = max(blk * RB, kk * P), min((blk + 1) * RB, (kk + 1) * P)
            c0, c1 = max(blk * RB, m * P), min((blk + 1) * RB, (m + 1) * P)
            if r0 < r1 and c0 < c1:
                w = a["rg_w_x" if g else "rg_w_a"]
                band[:, r0 - kk * P:r1 - kk * P, n * P + c0 - m * P:n * P + c1 - m * P] = \
                    w[:, blk, r0 - blk * RB:r1 - blk * RB, c0 - blk * RB:c1 - blk * RB]
    rel = a["rel_table"][:, :, ::-1].reshape(DEPTH * HEADS, RELW)
    arrays = {
        "x": a["x"], "w_gate1": a["ffn1_w_gate"], "w_up1": a["ffn1_w_up"], "w_down1": a["ffn1_w_down"],
        "w_in": a["w_in"], "rg_band": band, "w_up_a": a["w_up_a"], "w_up_b": a["w_up_b"], "w_out": a["w_out"],
        "w_gate2": a["ffn2_w_gate"], "w_up2": a["ffn2_w_up"], "w_down2": a["ffn2_w_down"], "params": params,
        "rel_rev": rel, "first_gain": tiles(a["norm_ffn1"])[0],
    }
    arrays = {f"in_{n}": np.ascontiguousarray(v) for n, v in arrays.items()}
    nc = bacc.Bacc("TRN2", target_bir_lowering=False, num_devices=1)
    args = [nc.dram_tensor(n, v.shape, mybir.dt.from_np(v.dtype), kind="ExternalInput").ap()
            for n, v in arrays.items()]
    args.append(nc.dram_tensor("out", (1, S, D), F32, kind="ExternalOutput").ap())
    trunk(nc, *args)
    return run(nc, [arrays], core_ids=[0]).results[0]["out"]
```
